# Optimizing a Trainium2 kernel written in Bass

```python
import jax, jax.numpy as jnp
from jax import lax
import numpy as np

D_MODEL = 2048
BATCH = 1
SEQ = 256
DEPTH = 2
DEC_BATCH = 8
DEC_SEQ = 1
PAST_LEN = 2048
PAGE_SIZE = 128

N_HEADS = 16
N_KV = 4
HEAD_DIM = 64
GQA = N_HEADS // N_KV
WINDOW = 128
ATTN_BLOCK = WINDOW
ROPE_THETA = 10000.0
CONV_DIM = D_MODEL // 2
CONV_WIDTH = 3
CHUNK = 128
CMLP_W = D_MODEL
CMLP_GROUPS = 16
CMLP_DG = CMLP_W // CMLP_GROUPS
FFN_W = 4 * D_MODEL
Q_W = N_HEADS * HEAD_DIM
KV_W = N_KV * HEAD_DIM
EVEN_PROJ = Q_W + 2 * KV_W + 3 * CONV_DIM
EVEN_CAT = Q_W + CONV_DIM
N_EVEN = (DEPTH + 1) // 2
N_ODD = DEPTH // 2
EPS = 1e-6

kernel_name = 'sink_swa_shortconv_chunkgmlp_step'

def rmsnorm(x, g):
    xf = x.astype(jnp.float32)
    y = xf * lax.rsqrt(jnp.mean(xf * xf, axis=-1, keepdims=True) + EPS)
    return (y * g.astype(jnp.float32)).astype(x.dtype)

def layernorm(x, g, b):
    xf = x.astype(jnp.float32)
    xc = xf - jnp.mean(xf, axis=-1, keepdims=True)
    var = jnp.mean(xc * xc, axis=-1, keepdims=True)
    return (xc * lax.rsqrt(var + EPS) * g.astype(jnp.float32) + b.astype(jnp.float32)).astype(x.dtype)

def rope(x, pos):
    half = HEAD_DIM // 2
    inv_freq = ROPE_THETA ** (-jnp.arange(half, dtype=jnp.float32) / half)
    ang = pos.astype(jnp.float32)[:, None] * inv_freq[None, :]
    cos = jnp.cos(ang)[:, None, :]
    sin = jnp.sin(ang)[:, None, :]
    xf = x.astype(jnp.float32)
    x1, x2 = xf[..., :half], xf[..., half:]
    return jnp.concatenate([x1 * cos - x2 * sin, x2 * cos + x1 * sin], axis=-1).astype(x.dtype)

def sink_softmax(scores, mask, sink):
    s = jnp.where(mask, scores, -jnp.inf)
    m = jnp.maximum(jnp.max(s, axis=-1, keepdims=True), sink)
    p = jnp.exp(s - m)
    return p / (jnp.sum(p, axis=-1, keepdims=True) + jnp.exp(sink - m))

def split_even(p):
    cuts = [Q_W, Q_W + KV_W, Q_W + 2 * KV_W, Q_W + 2 * KV_W + CONV_DIM, Q_W + 2 * KV_W + 2 * CONV_DIM]
    return jnp.split(p, cuts, axis=-1)

def causal_conv(zcat, w):
    t = zcat.shape[1] - (CONV_WIDTH - 1)
    out = w[0] * zcat[:, 0:t]
    for i in range(1, CONV_WIDTH):
        out = out + w[i] * zcat[:, i:i + t]
    return out

def window_attn_prompt(q, k, v, sinks):
    b, s = q.shape[:2]
    nb = s // ATTN_BLOCK
    qb = q.reshape(b, nb, ATTN_BLOCK, N_KV, GQA, HEAD_DIM)
    kb = k.reshape(b, nb, ATTN_BLOCK, N_KV, HEAD_DIM)
    vb = v.reshape(b, nb, ATTN_BLOCK, N_KV, HEAD_DIM)
    zk = jnp.zeros_like(kb[:, :1])
    kband = jnp.concatenate([jnp.concatenate([zk, kb[:, :-1]], axis=1), kb], axis=2)
    vband = jnp.concatenate([jnp.concatenate([zk, vb[:, :-1]], axis=1), vb], axis=2)
    scores = jnp.einsum('bnqkgd,bnskd->bnkgqs', qb, kband).astype(jnp.float32) * (HEAD_DIM ** -0.5)
    blk = jnp.arange(nb)[:, None] * ATTN_BLOCK
    qpos = blk + jnp.arange(ATTN_BLOCK)[None, :]
    kpos = blk - ATTN_BLOCK + jnp.arange(2 * ATTN_BLOCK)[None, :]
    diff = qpos[:, :, None] - kpos[:, None, :]
    mask = (diff >= 0) & (diff < WINDOW) & (kpos[:, None, :] >= 0)
    sink = sinks.astype(jnp.float32).reshape(N_KV, GQA)[None, None, :, :, None, None]
    probs = sink_softmax(scores, mask[None, :, None, None], sink)
    out = jnp.einsum('bnkgqs,bnskd->bnqkgd', probs.astype(v.dtype), vband)
    return out.reshape(b, s, Q_W)

def window_attn_sample(q, kall, vall, sinks):
    dbs, t = q.shape[:2]
    qg = q.reshape(dbs, t, N_KV, GQA, HEAD_DIM)
    scores = jnp.einsum('btkgd,bskd->bkgts', qg, kall).astype(jnp.float32) * (HEAD_DIM ** -0.5)
    qpos = PAST_LEN + jnp.arange(t)
    kpos = PAST_LEN - WINDOW + jnp.arange(WINDOW + t)
    diff = qpos[:, None] - kpos[None, :]
    mask = (diff >= 0) & (diff < WINDOW)
    sink = sinks.astype(jnp.float32).reshape(N_KV, GQA)[None, :, :, None, None]
    probs = sink_softmax(scores, mask[None, None, None], sink)
    out = jnp.einsum('bkgts,bskd->btkgd', probs.astype(vall.dtype), vall)
    return out.reshape(dbs, t, Q_W)

def even_prompt(h, w_in, w_out, conv_w, sinks):
    b, s, _ = h.shape
    q, k, v, gate_b, gate_c, h_conv = split_even(h @ w_in)
    pos = jnp.arange(s)
    q = rope(q.reshape(b, s, N_HEADS, HEAD_DIM), pos)
    k = rope(k.reshape(b, s, N_KV, HEAD_DIM), pos)
    v = v.reshape(b, s, N_KV, HEAD_DIM)
    attn = window_attn_prompt(q, k, v, sinks)
    z = gate_c * h_conv
    zcat = jnp.concatenate([jnp.zeros((b, CONV_WIDTH - 1, CONV_DIM), z.dtype), z], axis=1)
    conv = gate_b * causal_conv(zcat, conv_w)
    out = jnp.concatenate([attn, conv], axis=-1) @ w_out
    return out, k[:, s - WINDOW:], v[:, s - WINDOW:], z[:, s - (CONV_WIDTH - 1):]

def even_sample(h, cache_k, cache_v, conv_state, w_in, w_out, conv_w, sinks):
    dbs, t, _ = h.shape
    q, k, v, gate_b, gate_c, h_conv = split_even(h @ w_in)
    pos = PAST_LEN + jnp.arange(t)
    q = rope(q.reshape(dbs, t, N_HEADS, HEAD_DIM), pos)
    k = rope(k.reshape(dbs, t, N_KV, HEAD_DIM), pos)
    v = v.reshape(dbs, t, N_KV, HEAD_DIM)
    kall = jnp.concatenate([cache_k, k], axis=1)
    vall = jnp.concatenate([cache_v, v], axis=1)
    attn = window_attn_sample(q, kall, vall, sinks)
    z = gate_c * h_conv
    zcat = jnp.concatenate([conv_state, z], axis=1)
    conv = gate_b * causal_conv(zcat, conv_w)
    out = jnp.concatenate([attn, conv], axis=-1) @ w_out
    return out, kall[:, t:], vall[:, t:], zcat[:, t:]

def cmlp_uv(h, w_in, ln_g, ln_b):
    z = jax.nn.gelu(h @ w_in, approximate=False)
    u, v = jnp.split(z, 2, axis=-1)
    return u, layernorm(v, ln_g, ln_b)

def cmlp_prompt(h, w_in, w_out, ln_g, ln_b, w_s, b_s):
    b, s, _ = h.shape
    nc = s // CHUNK
    u, v = cmlp_uv(h, w_in, ln_g, ln_b)
    vg = v.reshape(b, nc, CHUNK, CMLP_GROUPS, CMLP_DG)
    ws = jnp.tril(w_s)
    mix = jnp.einsum('gts,bnsgd->bntgd', ws, vg) + b_s.T[None, None, :, :, None]
    gated = u.reshape(b, nc, CHUNK, CMLP_GROUPS, CMLP_DG) * mix
    return gated.reshape(b, s, CMLP_W) @ w_out, v[:, s - CHUNK:]

def cmlp_sample(h, w_in, w_out, ln_g, ln_b, w_s, b_s):
    dbs, t, _ = h.shape
    u, v = cmlp_uv(h, w_in, ln_g, ln_b)
    vg = v.reshape(dbs, t, CMLP_GROUPS, CMLP_DG)
    ws = jnp.tril(w_s[:, :t, :t])
    mix = jnp.einsum('gts,bsgd->btgd', ws, vg) + b_s[:, :t].T[None, :, :, None]
    gated = u.reshape(dbs, t, CMLP_GROUPS, CMLP_DG) * mix
    return gated.reshape(dbs, t, CMLP_W) @ w_out, v

def ffn(h, w_up, w_down):
    a = jax.nn.relu(h @ w_up)
    return (a * a) @ w_down

def setup_inputs(seed: int = 0) -> dict:
    key = jax.random.key(seed)
    ks = jax.random.split(key, 21)

    def nrm(k, shape, scale):
        return jax.random.normal(k, shape, jnp.float32) * scale

    return {
        'x_prompt': nrm(ks[0], (BATCH, SEQ, D_MODEL), 1.0),
        'x_sample': nrm(ks[1], (DEC_BATCH, DEC_SEQ, D_MODEL), 1.0),
        'cache_k_win': nrm(ks[2], (N_EVEN, DEC_BATCH, WINDOW, N_KV, HEAD_DIM), 1.0),
        'cache_v_win': nrm(ks[3], (N_EVEN, DEC_BATCH, WINDOW, N_KV, HEAD_DIM), 1.0),
        'state_conv': nrm(ks[4], (N_EVEN, DEC_BATCH, CONV_WIDTH - 1, CONV_DIM), 1.0),
        'w_in_even': nrm(ks[5], (N_EVEN, D_MODEL, EVEN_PROJ), D_MODEL ** -0.5),
        'w_out_even': nrm(ks[6], (N_EVEN, EVEN_CAT, D_MODEL), EVEN_CAT ** -0.5),
        'conv_w': nrm(ks[7], (N_EVEN, CONV_WIDTH, CONV_DIM), CONV_WIDTH ** -0.5),
        'attn_sinks': nrm(ks[8], (N_EVEN, N_HEADS), 0.5),
        'w_in_cmlp': nrm(ks[9], (N_ODD, D_MODEL, 2 * CMLP_W), D_MODEL ** -0.5),
        'w_out_cmlp': nrm(ks[10], (N_ODD, CMLP_W, D_MODEL), CMLP_W ** -0.5),
        'ln_v_g': 1.0 + nrm(ks[11], (N_ODD, CMLP_W), 0.1),
        'ln_v_b': nrm(ks[12], (N_ODD, CMLP_W), 0.02),
        'w_spatial': nrm(ks[13], (N_ODD, CMLP_GROUPS, CHUNK, CHUNK), CHUNK ** -0.5),
        'b_spatial': 1.0 + nrm(ks[14], (N_ODD, CMLP_GROUPS, CHUNK), 0.1),
        'w_ffn_up': nrm(ks[15], (DEPTH, D_MODEL, FFN_W), D_MODEL ** -0.5),
        'w_ffn_down': nrm(ks[16], (DEPTH, FFN_W, D_MODEL), FFN_W ** -0.5),
        'g_mix_pre': 1.0 + nrm(ks[17], (DEPTH, D_MODEL), 0.1),
        'g_mix_post': 1.0 + nrm(ks[18], (DEPTH, D_MODEL), 0.1),
        'g_ffn_pre': 1.0 + nrm(ks[19], (DEPTH, D_MODEL), 0.1),
        'g_ffn_post': 1.0 + nrm(ks[20], (DEPTH, D_MODEL), 0.1),
    }

def reference(x_prompt, x_sample, cache_k_win, cache_v_win, state_conv, w_in_even, w_out_even, conv_w,
              attn_sinks, w_in_cmlp, w_out_cmlp, ln_v_g, ln_v_b, w_spatial, b_spatial, w_ffn_up, w_ffn_down,
              g_mix_pre, g_mix_post, g_ffn_pre, g_ffn_post):
    xp, xs = x_prompt, x_sample
    kp_l, vp_l, cp_l, up_l = [], [], [], []
    ks_l, vs_l, cs_l, us_l = [], [], [], []
    for i in range(DEPTH):
        j = i // 2
        hp = rmsnorm(xp, g_mix_pre[i])
        hs = rmsnorm(xs, g_mix_pre[i])
        if i % 2 == 0:
            op, k_p, v_p, c_p = even_prompt(hp, w_in_even[j], w_out_even[j], conv_w[j], attn_sinks[j])
            osm, k_s, v_s, c_s = even_sample(hs, cache_k_win[j], cache_v_win[j], state_conv[j],
                                             w_in_even[j], w_out_even[j], conv_w[j], attn_sinks[j])
            kp_l.append(k_p); vp_l.append(v_p); cp_l.append(c_p)
            ks_l.append(k_s); vs_l.append(v_s); cs_l.append(c_s)
        else:
            op, r_p = cmlp_prompt(hp, w_in_cmlp[j], w_out_cmlp[j], ln_v_g[j], ln_v_b[j], w_spatial[j], b_spatial[j])
            osm, r_s = cmlp_sample(hs, w_in_cmlp[j], w_out_cmlp[j], ln_v_g[j], ln_v_b[j], w_spatial[j], b_spatial[j])
            up_l.append(r_p); us_l.append(r_s)
        xp = xp + rmsnorm(op, g_mix_post[i])
        xs = xs + rmsnorm(osm, g_mix_post[i])
        xp = xp + rmsnorm(ffn(rmsnorm(xp, g_ffn_pre[i]), w_ffn_up[i], w_ffn_down[i]), g_ffn_post[i])
        xs = xs + rmsnorm(ffn(rmsnorm(xs, g_ffn_pre[i]), w_ffn_up[i], w_ffn_down[i]), g_ffn_post[i])
    return (xp, xs, jnp.stack(kp_l), jnp.stack(vp_l), jnp.stack(cp_l), jnp.stack(up_l),
            jnp.stack(ks_l), jnp.stack(vs_l), jnp.stack(cs_l), jnp.stack(us_l))


_drawn_inputs = setup_inputs


def setup_inputs(seed=0):
    import zlib

    import numpy as np

    out = dict(_drawn_inputs(seed))
    spreads = {}
    factors = {'attn_sinks': 7.843, 'ln_v_b': 2.921}
    for name, (base, spread) in spreads.items():
        noise = np.random.default_rng([zlib.crc32(name.encode()), seed]).standard_normal(out[name].shape)
        drawn = base * np.exp(spread * noise) if base else spread * noise
        out[name] = __import__('jax').numpy.asarray(drawn.astype(out[name].dtype))
    for name, factor in factors.items():
        out[name] = (out[name] * factor).astype(out[name].dtype)
    return out
```

```python
from contextlib import ExitStack

import numpy as np

import concourse.bass as bass
from concourse import mybir

F32 = mybir.dt.float32
F32R = mybir.dt.float32r
ALU = mybir.AluOpType
ACT = mybir.ActivationFunctionType
AX = mybir.AxisListType

P = 128
D = 2048
CH = D // P
PAIRS = CH // 2
SEQ = 256
NB = 8
T = SEQ + NB
QT = SEQ // P
HD = 64
NH = 16
NKV = 4
GQA = NH // NKV
KVW = NKV * HD
CONV = 1024
CONVT = CONV // P
WIN = 128
FFN = 4 * D
FG = FFN // D
EPS = 1e-6
SCALE = HD ** -0.5
MASKED = -1e30

BC = 256
NQ = 4
QK = CH // NQ
UNIT = D // BC

N_EVEN = 0
N_EOUT = (NH * HD + 2 * KVW + 3 * CONV) // BC
N_FFN = [N_EOUT + UNIT, N_EOUT + UNIT + 2 * UNIT * FG + 3 * UNIT]
N_CIN = N_FFN[0] + 2 * UNIT * FG
N_COUT = N_CIN + 2 * UNIT
N_END = N_FFN[1] + 2 * UNIT * FG

N_K = NH * HD // BC
N_V = N_K + 1
N_CONV = N_V + 1
N_SAMP = N_CONV + 1
N_PR = N_SAMP + 2


def conv_col(n):
    i, part = divmod(n - N_CONV, 3)
    return N_CONV + (4, 8, 0)[part] + i


def even_col(n):
    return n if n < N_CONV else conv_col(n)


def build(nc, io):
    ctx = ExitStack()
    with ctx:
        def sb(name, shape, dt=F32):
            return ctx.enter_context(nc.sbuf_tensor(name, shape, dt))

        def sem(name):
            return ctx.enter_context(nc.semaphore(name))

        raw = sb("raw", [P, 4, 2 * QK, BC])
        whi = sb("whi", [P, CH, BC], F32R)
        wlo = sb("wlo", [P, CH, BC], F32R)
        x = sb("x", [P, CH, T])
        y = sb("y", [P, CH, T])
        hhi = sb("hhi", [P, CH, T], F32R)
        hlo = sb("hlo", [P, CH, T], F32R)
        ahi = sb("ahi", [P, CH, T], F32R)
        alo = sb("alo", [P, CH, T], F32R)
        ident = sb("ident", [P, P])
        mean_w = sb("mean_w", [P, P])
        cos = sb("cos", [P, T])
        sin = sb("sin", [P, T])
        rs_pre = sb("rs_pre", [P, T])
        rs_post = sb("rs_post", [P, T])
        var = sb("var", [P, T])
        tmp = sb("tmp", [P, T])
        acc_pre = sb("acc_pre", [P, 2, T])
        acc_post = sb("acc_post", [P, 2, T])
        sq = sb("sq", [P, 2, 2, T])
        sq_tail = sb("sq_tail", [P, 2, T])
        gains = sb("gains", [P, 8, CH])
        lnw = sb("lnw", [P, 2 * CH + 3 * CONVT])
        sinks = sb("sinks", [P, NH])
        small = sb("small", [P, 48])
        ln_g = lnw[:, 0:CH]
        ln_b = lnw[:, CH:2 * CH]
        conv_w = lnw[:, 2 * CH:].rearrange("p (w c) -> p w c", w=3)

        REGION = 10496
        region = sb("region", [P, REGION])

        def part(start, *dims):
            size = int(np.prod(dims))
            assert start + size <= REGION
            ap = region[:, start:start + size]
            names = "abc"[:len(dims)]
            if len(dims) == 1:
                return ap
            return ap.rearrange(f"p ({' '.join(names)}) -> p {' '.join(names)}", **dict(zip(names, dims)))

        x_tok = part(0, 3, D)
        g_rows = part(3 * D, 2, P)
        state_tok = part(3 * D + 2 * P, CONV)
        S = part(0, 2, 2, 2 * P)
        kt_win = part(0, 2, NKV, P)
        PT = part(1024, 2, 4, P)
        kv_new = part(1024, 2, KVW)
        kt2 = part(2048, NKV, SEQ)
        swp = part(2048, 2, T)
        KROW = KVW + HD
        k_tok = part(3072, QT, KROW)
        v_tok = part(3712, QT, KVW)
        k_win = part(4224, NB, KROW)
        v_win = part(6784, NB, KVW)
        sc_s = part(8832, P)
        p_s = part(8960, P)
        pt_s = part(9088, P)
        sink_r = part(9216, P)
        z = part(9344, 2, T + 2)
        z_last = part(9876, CONVT, 2 + NB)
        state_t = part(9956, CONVT, NB, 2)
        conv_s = part(10084, CONVT, NB)
        mask = part(10148, 2 * P)
        conv_t = part(10404, CONVT, NB)
        z_tok = part(0, CONV)
        q_t = y[:, 0:8, :]
        u = part(0, CH, T)
        ws_raw = part(0, CH, P)
        ws_t = part(4224, CH, P)
        b_bc = part(4224 + 2048, CH, P)
        ws00 = part(4224 + 4096, CH)
        vt = part(4224 + 4096 + CH, 2, 3, P)
        relu = part(9000, 2, T)
        asq = part(9528, 2, T)
        out_tok = part(0, 3, D)

        ps = ctx.enter_context(nc.psum_tensor("ps", [P, 8, 512], F32))

        def pair(par):
            return ps[:, 2 * par:2 * par + 2, 0:T]

        ps_s = ps[:, 4:6, :]
        ps_t = ps[:, 6, :]
        ps_v = ps[:, 7, :]
        ps_stat = ps[:, 7, 0:T]

        raw_loaded = [sem(f"raw_loaded{i}") for i in range(4)]
        w_hi_ready = sem("w_hi_ready")
        w_lo_ready = sem("w_lo_ready")
        w_used = sem("w_used")
        taken = sem("taken")
        x_in = [sem(f"x_in{i}") for i in range(3)]
        g_in = sem("g_in")
        l_in = sem("l_in")
        sinks_in = sem("sinks_in")
        rope_in = sem("rope_in")
        state_in = sem("state_in")
        win_in = sem("win_in")
        new_in = sem("new_in")
        win_ready = sem("win_ready")
        ws_in = sem("ws_in")
        bias_in = sem("bias_in")
        const_ready = sem("const_ready")
        g_turned = sem("g_turned")
        g_ready = sem("g_ready")
        x_turned = sem("x_turned")
        x_ready = sem("x_ready")
        h_hi_ready = sem("h_hi_ready")
        h_ready = sem("h_ready")
        sq_ready = sem("sq_ready")
        sq_used = sem("sq_used")
        tail_ready = sem("tail_ready")
        stat_ready = sem("stat_ready")
        var_ready = sem("var_ready")
        root_ready = sem("root_ready")
        scaled = sem("scaled")
        x_added = sem("x_added")
        x_added_v = sem("x_added_v")
        y_zero = sem("y_zero")
        chain = sem("chain")
        pool_chain = sem("pool_chain")
        asq_ready = sem("asq_ready")
        a_ready = sem("a_ready")
        swap_ready = sem("swap_ready")
        kv_turned = sem("kv_turned")
        kv_copied = sem("kv_copied")
        k2_turned = sem("k2_turned")
        k2_ready = sem("k2_ready")
        win_turned = sem("win_turned")
        win_copied = sem("win_copied")
        win_scored = sem("win_scored")
        sc_ready = sem("sc_ready")
        sc_turned = sem("sc_turned")
        s_max = sem("s_max")
        s_exp = sem("s_exp")
        s_prob = sem("s_prob")
        s_pturned = sem("s_pturned")
        s_pt = sem("s_pt")
        s_pv = sem("s_pv")
        s_hi = sem("s_hi")
        s_attn = sem("s_attn")
        scored = sem("scored")
        masked = sem("masked")
        p_exp = sem("p_exp")
        p_rec = sem("p_rec")
        p_norm = sem("p_norm")
        p_turned = sem("p_turned")
        p_copied = sem("p_copied")
        pv_done = sem("pv_done")
        attn_hi = sem("attn_hi")
        attn_ready = sem("attn_ready")
        mask_ready = sem("mask_ready")
        state_turned = sem("state_turned")
        state_ready = sem("state_ready")
        conv_s_ready = sem("conv_s_ready")
        z_ready = sem("z_ready")
        tap0_ready = sem("tap0_ready")
        conv_done = sem("conv_done")
        conv_hi = sem("conv_hi")
        conv_ready = sem("conv_ready")
        z_turned = sem("z_turned")
        z_out = sem("z_out")
        sink_ready = sem("sink_ready")
        sink_turned = sem("sink_turned")
        ws_masked = sem("ws_masked")
        ws_turned = sem("ws_turned")
        ws_ready = sem("ws_ready")
        gelu_ready = sem("gelu_ready")
        v_summed = sem("v_summed")
        centred = sem("centred")
        ln_scaled = sem("ln_scaled")
        v_ready = sem("v_ready")
        v_turned = sem("v_turned")
        v_copied = sem("v_copied")
        v_stored = [sem(f"v_stored{i}") for i in range(2)]
        mixed = sem("mixed")
        mix_ready = sem("mix_ready")
        gated_ready = sem("gated_ready")
        gated_hi = sem("gated_hi")
        g_lo_ready = sem("g_lo_ready")
        y_turned = sem("y_turned")
        y_copied_a = sem("y_copied_a")
        y_copied_v = sem("y_copied_v")
        stored = sem("stored")
        kv_stored = sem("kv_stored")

        block = ctx.enter_context(nc.Block())

        def twice(ap):
            return ap.unsqueeze(1).to_broadcast([P, 2, ap.shape[-1]])

        def rows(w):
            return w.rearrange("(k p) n -> p k n", p=P)

        w_even = rows(io["w_in_even"][0])
        w_eout = rows(io["w_out_even"][0])
        w_cin = rows(io["w_in_cmlp"][0])
        w_cout = rows(io["w_out_cmlp"][0])
        w_up = [rows(io["w_ffn_up"][l]) for l in range(2)]
        w_down = [rows(io["w_ffn_down"][l]) for l in range(2)]

        SQ_X0, SQ_POST0, SQ_PRE1, SQ_POST1, SQ_PRE2, SQ_LN, SQ_POST2, SQ_PRE3, SQ_POST3 = (
            0, 8, 15, 23, 30, 38, 46, 53, 61)
        TAIL = PAIRS - 1
        ST_X0, ST_POST0, ST_PRE1, ST_POST1, ST_PRE2, ST_MEAN, ST_LN, ST_POST2, ST_PRE3, ST_POST3 = range(10)
        MIX_POST = {0: (SQ_POST0, ST_POST0), 1: (SQ_POST1, ST_POST1), 2: (SQ_POST2, ST_POST2), 3: (SQ_POST3, ST_POST3)}
        PRE = {0: (SQ_X0, ST_X0), 1: (SQ_PRE1, ST_PRE1), 2: (SQ_PRE2, ST_PRE2), 3: (SQ_PRE3, ST_PRE3)}
        G_PRE = {0: 0, 1: 4, 2: 1, 3: 5}
        G_POST = {0: 2, 1: 6, 2: 3, 3: 7}
        ROOTS = [ST_X0, ST_POST0, ST_POST1, ST_PRE2, ST_LN, ST_POST2, ST_POST3]

        GATED_AT = {3: (0, 1), 4: (2, 3), 5: (4,), 6: (5, 6), 7: (7,)}

        @block.sync
        def _(sp):
            def load(w, k0, c0, P2, par):
                for h in range(2):
                    if not (isinstance(P2, int) and P2 == 0):
                        sp.wait_ge(w_lo_ready, 8 * P2 + 4 * par - 8 + 2 * h + 2)
                    sp.dma_start(raw[:, 2 * par + h], w[:, bass.ds(k0 + 2 * QK * h, 2 * QK), bass.ds(c0, BC)]
                                 ).then_inc(raw_loaded[2 * par + h], 16)

            for t in range(QT):
                sp.dma_start(x_tok[:, t, :], io["x_prompt"][0, t * P:(t + 1) * P, :]).then_inc(x_in[t], 16)
            sp.dma_start(x_tok[0:NB, 2, :], io["x_sample"][:, 0, :]).then_inc(x_in[2], 16)
            sp.dma_start(g_rows[0:CH, 1, :], io["ln_v_g"].rearrange("l (c p) -> (l c) p", p=P)).then_inc(l_in, 16)
            sp.dma_start(g_rows[CH:2 * CH, 1, :], io["ln_v_b"].rearrange("l (c p) -> (l c) p", p=P)).then_inc(l_in, 16)
            sp.dma_start(g_rows[2 * CH:2 * CH + 3 * CONVT, 1, :],
                         io["conv_w"][0].rearrange("w (c p) -> (w c) p", p=P)).then_inc(l_in, 16)
            for n in range(N_EOUT):
                load(w_even, 0, BC * even_col(n), n // 2, n % 2)
                if n == 1:
                    sp.dma_start(cos[:, :], io["rope_cos"]).then_inc(rope_in, 16)
                    sp.dma_start(sin[:, :], io["rope_sin"]).then_inc(rope_in, 16)
                if n == N_K:
                    sp.wait_ge(x_ready, PAIRS)
                    sp.wait_ge(state_ready, 1)
                    for win, cache in ((k_win, io["cache_k_win"]), (v_win, io["cache_v_win"])):
                        for lo, hi in ((0, 112), (112, P - 1)):
                            sp.dma_start(win[lo:hi, :, 0:KVW], cache[0, :, 1 + lo:1 + hi].rearrange("b s g d -> s b (g d)")
                                         ).then_inc(win_in, 16)
            with sp.Fori(0, UNIT // 2) as i:
                for par in range(2):
                    load(w_eout, 0, 2 * BC * i + BC * par, N_EOUT // 2 + i, par)

            def ffn(l, n0):
                with sp.Fori(0, FG) as j:
                    with sp.Fori(0, UNIT // 2) as i:
                        for par in range(2):
                            load(w_up[l], 0, D * j + 2 * BC * i + BC * par, n0 // 2 + UNIT * j + i, par)
                    with sp.Fori(0, UNIT // 2) as i:
                        for par in range(2):
                            load(w_down[l], CH * j, 2 * BC * i + BC * par, n0 // 2 + UNIT // 2 + UNIT * j + i, par)

            ffn(0, N_FFN[0])
            for half in range(2):
                with sp.Fori(0, UNIT // 2) as i:
                    for par in range(2):
                        load(w_cin, 0, D * (1 - half) + 2 * BC * i + BC * par, (N_CIN + UNIT * half) // 2 + i, par)
            with sp.Fori(0, UNIT // 2) as i:
                for par in range(2):
                    load(w_cout, 0, 2 * BC * i + BC * par, N_COUT // 2 + i, par)
            ffn(1, N_FFN[1])
            for c in range(4):
                cols = slice(512 * c, 512 * c + 512)
                sp.wait_ge(y_copied_a, 2 * c + 2)
                sp.wait_ge(y_copied_v, c + 1)
                for t in range(QT):
                    sp.dma_start(io["y_prompt"][0, t * P:(t + 1) * P, cols], out_tok[:, t, cols]).then_inc(stored, 16)
                sp.dma_start(io["y_sample"][:, 0, cols], out_tok[0:NB, 2, cols]).then_inc(stored, 16)
            sp.wait_ge(stored, 16 * 12)

        @block.gpsimd
        def _(pool):
            done = [0]

            def step(ins):
                done[0] += 1
                ins.then_inc(pool_chain, 1)
                pool.wait_ge(pool_chain, done[0])

            step(pool.memset(ident[:, :], 0.0))
            pool.affine_select(out=ident[:, :], in_=ident[:, :], compare_op=ALU.not_equal, fill=1.0, base=0,
                               pattern=[[-1, P]], channel_multiplier=1).then_inc(const_ready, 1)
            pool.memset(mean_w[:, :], 1.0 / D).then_inc(const_ready, 1)

            def sum_squares(acc, s0, count=PAIRS):
                for s in range(s0, s0 + count):
                    pool.wait_ge(sq_ready, s + 1)
                    if s == s0:
                        pool.tensor_copy(acc[:, :, :], sq[:, s % 2]).then_inc(sq_used, 1)
                    else:
                        pool.wait_ge(sq_used, s)
                        pool.tensor_tensor(acc[:, :, :], acc[:, :, :], sq[:, s % 2], ALU.add).then_inc(sq_used, 1)

            def residual(k, mine=range(PAIRS)):
                sum_squares(acc_post, MIX_POST[k][0], TAIL)
                for c in mine:
                    pool.wait_ge(scaled, PAIRS * k + c + 1)
                    pool.tensor_tensor(x[:, 2 * c:2 * c + 2, :], x[:, 2 * c:2 * c + 2, :], y[:, 2 * c:2 * c + 2, :],
                                       ALU.add).then_inc(x_added, 1)
                if k in (0, 2):
                    pool.wait_ge(x_added, PAIRS * k + PAIRS)
                    pool.memset(y[:, :, :], 0.0).then_inc(y_zero, 1)

            sum_squares(acc_pre, SQ_X0)
            pool.wait_ge(x_ready, PAIRS)
            pool.wait_ge(state_ready, 1)
            step(pool.memset(mask[:, :], 0.0))
            step(pool.affine_select(out=mask[:, 0:P], in_=mask[:, 0:P], compare_op=ALU.is_gt, fill=MASKED, base=0,
                                    pattern=[[1, P]], channel_multiplier=-1))
            pool.affine_select(out=mask[:, P:2 * P], in_=mask[:, P:2 * P], compare_op=ALU.is_ge, fill=MASKED,
                               base=0, pattern=[[-1, P]], channel_multiplier=1).then_inc(mask_ready, 1)
            step(pool.memset(z[:, :, 0:2], 0.0))
            for tap in range(2):
                w = conv_w[:, tap, :].unsqueeze(2).to_broadcast([P, CONVT, NB])
                step(pool.tensor_tensor((conv_s if tap == 0 else conv_t)[:, :, :], state_t[:, :, :, tap], w, ALU.mult))
            pool.tensor_tensor(conv_s[:, :, :], conv_s[:, :, :], conv_t[:, :, :], ALU.add).then_inc(conv_s_ready, 1)
            pool.wait_ge(new_in, 32)
            pool.tensor_copy(k_win[:, :, KVW:], k_win[:, :, 0:HD]).then_inc(win_ready, 1)
            for n in range(N_CONV, N_EOUT):
                if N_PR <= n < N_PR + 8:
                    it = n - N_PR
                    w = (1 + it % 2) * P
                    pool.wait_ge(p_rec, it + 1)
                    rec = small[:, 16:20].rearrange("p (a b) -> p a b", a=2)
                    for e in range(2):
                        ins = pool.tensor_tensor(S[:, e, :, 0:w], S[:, e, :, 0:w],
                                                 rec[:, e, :].unsqueeze(2).to_broadcast([P, 2, w]), ALU.mult)
                    ins.then_inc(p_norm, 1)
                i, kind = divmod(n - N_CONV, 3)
                if kind == 1:
                    pool.wait_ge(taken, n + 1)
                    if i:
                        pool.wait_ge(conv_done, i)
                    step(pool.tensor_tensor(z[:, :, 2:], y[:, 8:10, :], y[:, 10:12, :], ALU.mult))
                    pool.tensor_copy(z_last[:, 2 * i:2 * i + 2, :], z[:, :, SEQ:]).then_inc(z_ready, 1)
            residual(0)
            pool.wait_ge(ws_in, 16)
            pool.affine_select(out=ws_raw[:, :, :], in_=ws_raw[:, :, :], compare_op=ALU.is_ge, fill=0.0, base=0,
                               pattern=[[0, CH], [-1, P]], channel_multiplier=1).then_inc(ws_masked, 1)
            sum_squares(acc_pre, SQ_PRE1)
            residual(1)
            sum_squares(acc_pre, SQ_PRE2)
            for c in range(PAIRS):
                pool.wait_ge(gelu_ready, c + 1)
                src = y[:, 2 * c:2 * c + 2, :]
                if c == 0:
                    pool.tensor_copy(acc_post[:, :, :], src).then_inc(v_summed, 1)
                else:
                    pool.wait_ge(v_summed, c)
                    pool.tensor_tensor(acc_post[:, :, :], acc_post[:, :, :], src, ALU.add).then_inc(v_summed, 1)
            sum_squares(acc_pre, SQ_LN)
            residual(2)
            sum_squares(acc_pre, SQ_PRE3)
            residual(3, range(0, PAIRS, 2))

        @block.scalar
        def _(act):
            roots = [0]

            def root():
                roots[0] += 1
                act.wait_ge(var_ready, roots[0])
                act.activation(tmp[:, :], var[:, :], ACT.Sqrt).then_inc(root_ready, 1)

            def w_hi(P2, par, q):
                first = isinstance(P2, int) and P2 == 0 and par == 0
                if q % 2 == 0:
                    act.wait_ge(raw_loaded[2 * par + q // 2], 16 * P2 + 16)
                if not first:
                    act.wait_ge(w_used, 8 * P2 + 4 * par - 4 + q + 1)
                k = slice(QK * (q % 2), QK * (q % 2) + QK)
                act.activation(whi[:, QK * q:QK * q + QK, :], raw[:, 2 * par + q // 2, k, :], ACT.Copy
                               ).then_inc(w_hi_ready, 1)

            def next_hi(P2, par, qs=range(NQ)):
                for q in qs:
                    w_hi(P2 + par, 1 - par, q)

            def square_y(n, par, k, i):
                s = MIX_POST[k][0] + i
                act.wait_ge(taken, n + 1)
                if isinstance(i, int) and i == TAIL:
                    act.activation(sq_tail[:, :, :], y[:, 2 * i:2 * i + 2, :], ACT.Square).then_inc(tail_ready, 1)
                    return
                act.wait_ge(sq_used, s - 1)
                act.activation(sq[:, (MIX_POST[k][0] + par) % 2], y[:, bass.ds(2 * i, 2), :], ACT.Square
                               ).then_inc(sq_ready, 1)

            def hi_pair(k, c, src_sem, src_n):
                act.wait_ge(src_sem, src_n)
                for t in (2 * c, 2 * c + 1):
                    ins = act.activation(hhi[:, t, :], x[:, t, :], ACT.Copy, scale=gains[:, G_PRE[k], t:t + 1])
                ins.then_inc(h_hi_ready, 1)

            def square_x(k, c):
                s = PRE[k][0] + c
                if s >= 2:
                    act.wait_ge(sq_used, s - 1)
                act.activation(sq[:, s % 2], x[:, 2 * c:2 * c + 2, :], ACT.Square).then_inc(sq_ready, 1)

            def norm_residual(k):
                root()
                for c in range(PAIRS):
                    hi_pair(k + 1, c, x_added, PAIRS * k + c + 1)

            for n, name in enumerate(["g_mix_pre", "g_mix_post", "g_ffn_pre", "g_ffn_post"]):
                act.dma_start(g_rows[32 * n:32 * n + 32, 0, :],
                              io[name].rearrange("l (c p) -> (l c) p", p=P)).then_inc(g_in, 16)
            act.dma_start(state_tok[0:2 * NB, :], io["state_conv"][0].rearrange("b r n -> (b r) n")
                          ).then_inc(state_in, 16)
            act.dma_start(sinks[:, :], io["attn_sinks"][0].partition_broadcast(P)).then_inc(sinks_in, 16)

            act.wait_ge(g_turned, 1)
            act.activation(gains[:, :, :].rearrange("p a b -> p (a b)"), ps[:, 6, 0:P], ACT.Copy).then_inc(g_ready, 1)
            act.wait_ge(g_ready, 1)
            for c in range(PAIRS):
                hi_pair(0, c, x_ready, c + 1)
                if c < NQ:
                    w_hi(0, 0, c)
                if c:
                    square_x(0, c - 1)
            square_x(0, PAIRS - 1)
            next_hi(0, 0, (0, 1))
            act.wait_ge(state_turned, 1)
            act.activation(lnw[:, :], ps[:, 7, 0:2 * CH + 3 * CONVT], ACT.Copy).then_inc(g_ready, 1)
            act.activation(state_t.rearrange("p c b r -> p (c b r)"), ps[:, 4, 0:P], ACT.Copy).then_inc(state_ready, 1)
            act.dma_start(io["new_conv_sample"][0, :, 0, :], io["state_conv"][0, :, 1, :]).then_inc(kv_stored, 16)
            next_hi(0, 0, (2, 3))
            root()

            def even_task(n, q):
                if (n, q) == (N_CONV, 1):
                    act.wait_ge(kv_turned, 1)
                    keys = ps[:, 4, :].rearrange("p (a b) -> p a b", a=QT)
                    act.activation(k_tok[:, :, 0:KVW], keys, ACT.Copy).then_inc(kv_copied, 1)
                    act.activation(k_tok[:, :, KVW:], keys[:, :, 0:HD], ACT.Copy).then_inc(kv_copied, 1)
                    act.activation(v_tok.rearrange("p a b -> p (a b)"), ps[:, 5, :], ACT.Copy).then_inc(kv_copied, 1)
                    act.activation(kv_new[0:NB].rearrange("p a b -> p (a b)"), ps[0:NB, 6, :], ACT.Copy
                                   ).then_inc(kv_copied, 1)
                    act.wait_ge(kv_copied, 4)
                    act.wait_ge(win_in, 64)
                    act.dma_start(k_win[P - 1:P, :, 0:KVW], kv_new[0:NB, 0, :]).then_inc(new_in, 16)
                    act.dma_start(v_win[P - 1:P, :, :], kv_new[0:NB, 1, :]).then_inc(new_in, 16)
                    act.dma_start(io["new_k_win_prompt"][0, 0].rearrange("s g d -> s (g d)"), k_tok[:, QT - 1, 0:KVW]
                                  ).then_inc(kv_stored, 16)
                    act.dma_start(io["new_v_win_prompt"][0, 0].rearrange("s g d -> s (g d)"), v_tok[:, QT - 1, :]
                                  ).then_inc(kv_stored, 16)
                if (n, q) == (N_CONV, 3):
                    act.wait_ge(k2_turned, 1)
                    act.activation(kt2.rearrange("p a b -> p (a b)"), ps_s.rearrange("p a b -> p (a b)"), ACT.Copy
                                   ).then_inc(k2_ready, 1)
                if N_SAMP <= n < N_SAMP + 2:
                    b = NQ * (n - N_SAMP) + q
                    act.wait_ge(win_turned, b + 1)
                    if b >= 2:
                        act.wait_ge(win_scored, b - 1)
                    act.activation(kt_win[:, b % 2], ps_t.rearrange("p (a b) -> p a b", a=NKV), ACT.Copy
                                   ).then_inc(win_copied, 1)
                    if b == 0:
                        act.wait_ge(new_in, 32)
                        act.dma_start(io["new_k_win_sample"][0].rearrange("b s g d -> s b (g d)"), k_win[:, :, 0:KVW]
                                      ).then_inc(kv_stored, 16)
                        act.dma_start(io["new_v_win_sample"][0].rearrange("b s g d -> s b (g d)"), v_win[:, :, :]
                                      ).then_inc(kv_stored, 16)
                if (n, q) == (N_PR, 2):
                    act.wait_ge(s_max, 1)
                    act.activation(p_s[:, :], ps_t[:, 0:P], ACT.Exp, bias=small[:, 1:2], accum_out=small[:, 3:4]
                                   ).then_inc(s_exp, 1)
                    act.activation(small[:, 4:5], small[:, 2:3], ACT.Exp).then_inc(s_exp, 1)
                if (n, q) == (N_PR + 1, 0):
                    act.wait_ge(s_pturned, 1)
                    act.activation(pt_s[:, :], ps_t[:, 0:P], ACT.Copy).then_inc(s_pt, 1)
                if (n, q) == (N_PR + 2, 0):
                    act.wait_ge(s_pv, 1)
                    act.activation(ahi[:, 0:8, SEQ:], ps_v[:, 0:8 * NB].rearrange("p (a b) -> p a b", a=8), ACT.Copy
                                   ).then_inc(s_hi, 1)
                if q == 2 and N_PR <= n < N_PR + 8:
                    it = n - N_PR
                    w = (1 + it % 2) * P
                    act.wait_ge(masked, it + 1)
                    for e in range(2):
                        for jj in range(2):
                            j = 2 * e + jj
                            ins = act.activation(S[:, e, jj, 0:w], S[:, e, jj, 0:w], ACT.Exp,
                                                 bias=small[:, 12 + j:13 + j], accum_out=small[:, 24 + j:25 + j])
                    act.activation(small[:, 28:32], small[:, 20:24], ACT.Exp).then_inc(p_exp, 1)
                if q in (1, 2) and N_PR < n < N_PR + 9:
                    it = n - N_PR - 1
                    kb = q - 1
                    if kb == 0 or it % 2:
                        act.wait_ge(p_turned, it // 2 * 3 + (it % 2) + kb + 1)
                        if kb == 0 and it:
                            act.wait_ge(pv_done, it)
                        act.activation(PT[:, kb], ps_t.rearrange("p (a b) -> p a b", a=4), ACT.Copy
                                       ).then_inc(p_copied, 1)
                if q == 3 and N_PR < n < N_PR + 9:
                    it = n - N_PR - 1
                    g, qi = divmod(it, 2)
                    act.wait_ge(pv_done, it + 1)
                    act.activation(ahi[:, 2 * g:2 * g + 2, qi * P:qi * P + P],
                                   ps_v[:, 0:2 * P].rearrange("p (a b) -> p a b", a=2), ACT.Copy).then_inc(attn_hi, 1)

            for n in range(N_EOUT):
                for q in range(NQ if n else 0):
                    next_hi(n // 2, n % 2, (q,))
                    even_task(n, q)
                if n < N_V:
                    act.wait_ge(w_used, 4 * n + 4)
                    if n:
                        act.wait_ge(taken, n)
                    for s in range(4):
                        ins = act.activation(swp[32 * s:32 * s + 32], pair(n % 2)[32 * (s ^ 1):32 * (s ^ 1) + 32],
                                             ACT.Copy)
                    ins.then_inc(swap_ready, 1)
                i, kind = divmod(n - N_CONV, 3)
                if n >= N_CONV and kind == 2:
                    act.wait_ge(z_ready, i + 1)
                    if i:
                        act.wait_ge(conv_ready, i)
                    for t in range(2):
                        ins = act.activation(y[:, 14 + t, 0:SEQ], z[:, t, 0:SEQ], ACT.Copy,
                                             scale=conv_w[:, 0, 2 * i + t:2 * i + t + 1])
                    ins.then_inc(tap0_ready, 1)
                    act.wait_ge(conv_done, i + 1)
                    act.activation(ahi[:, 8 + 2 * i:10 + 2 * i, :], y[:, 14:16, :], ACT.Copy).then_inc(conv_hi, 1)

            def product_with_norm(n0, k, followed=True):
                with act.Fori(0, UNIT // 2 - 1) as i:
                    for par in range(2):
                        next_hi(n0 // 2 + i, par)
                        square_y(n0 + 2 * i + par, par, k, 2 * i + par)
                n = n0 + UNIT - 2
                next_hi(n // 2, 0)
                square_y(n, 0, k, UNIT - 2)
                if followed:
                    next_hi(n // 2, 1, (0, 1, 2))
                square_y(n + 1, 1, k, UNIT - 1)
                if followed:
                    next_hi(n // 2, 1, (3,))

            def up_blocks(P0, k=None):
                with act.Fori(0, UNIT // 2) as i:
                    for par in range(2):
                        next_hi(P0 + i, par, (0,))
                        if k is not None:
                            s0 = PRE[k][0]
                            act.wait_ge(sq_used, s0 + 2 * i + par - 1)
                            act.activation(sq[:, (s0 + par) % 2], x[:, bass.ds(4 * i + 2 * par, 2), :], ACT.Square
                                           ).then_inc(sq_ready, 1)
                        next_hi(P0 + i, par, (1, 2, 3))
                        act.wait_ge(taken, 2 * (P0 + i) + par + 1)
                        act.activation(asq[:, :, :], relu[:, :, :], ACT.Square).then_inc(asq_ready, 1)
                        act.activation(ahi[:, bass.ds(4 * i + 2 * par, 2), :], relu[:, :, :], ACT.Square
                                       ).then_inc(asq_ready, 1)

            def ws_copy(r):
                act.wait_ge(ws_turned, r + 1)
                act.activation(ws_t[:, 8 * r:8 * r + 8, :].rearrange("p a b -> p (a b)"),
                               ps_s.rearrange("p a b -> p (a b)"), ACT.Copy).then_inc(ws_ready, 1)
                if r:
                    act.activation(ws00[:, :], ps[:, 6, 0:CH], ACT.Copy, scale=float(D)).then_inc(ws_ready, 1)

            def ffn(l, n0, last):
                P0 = n0 // 2
                with act.Fori(0, FG - 1) as j:
                    up_blocks(P0 + UNIT * j)
                    with act.Fori(0, UNIT // 2) as i:
                        for par in range(2):
                            next_hi(P0 + UNIT * j + UNIT // 2 + i, par)
                if l == 0:
                    ws_copy(0)
                P0 = P0 + UNIT * (FG - 1)
                up_blocks(P0, 2 * l + 1)
                if l == 0:
                    ws_copy(1)
                product_with_norm(2 * P0 + UNIT, 2 * l + 1, not last)

            product_with_norm(N_EOUT, 0)
            norm_residual(0)
            act.wait_ge(z_turned, 1)
            act.activation(z_tok[0:2 + NB, :], ps[0:2 + NB, 4:6, :].rearrange("p a b -> p (a b)"), ACT.Copy
                           ).then_inc(z_out, 1)
            act.wait_ge(z_out, 1)
            act.dma_start(io["new_conv_prompt"][0, 0], z_tok[0:2, :]).then_inc(kv_stored, 16)
            act.dma_start(io["new_conv_sample"][0, :, 1, :], z_tok[2:2 + NB, :]).then_inc(kv_stored, 16)
            act.wait_ge(kv_stored, 16 * 7)
            act.wait_ge(s_attn, 1)
            act.wait_ge(attn_ready, 8)
            act.dma_start(ws_raw[:, :, :], io["w_spatial"][0].rearrange("g t s -> t g s")).then_inc(ws_in, 16)
            act.dma_start(b_bc[:, :, :], io["b_spatial"][0].partition_broadcast(P)).then_inc(bias_in, 16)

            ffn(0, N_FFN[0], False)
            norm_residual(1)

            def gelu_v(n, i):
                act.wait_ge(taken, n + 1)
                act.activation(y[:, bass.ds(2 * i, 2), :], y[:, bass.ds(2 * i, 2), :], ACT.Gelu).then_inc(gelu_ready, 1)

            for c in range(PAIRS):
                square_x(2, c)
                if c < NQ:
                    next_hi(N_CIN // 2, 0, (c,))
            root()
            gelu_v(N_CIN, 0)
            next_hi(N_CIN // 2, 1)
            gelu_v(N_CIN + 1, 1)
            with act.Fori(1, UNIT // 2) as i:
                for par in range(2):
                    next_hi(N_CIN // 2 + i, par)
                    gelu_v(N_CIN + 2 * i + par, 2 * i + par)
            for b in range(UNIT):
                n = N_CIN + UNIT + b
                for q in range(NQ):
                    g = NQ * (b - 2) + q
                    if 0 <= g < CH:
                        act.wait_ge(ln_scaled, g + 1)
                        act.activation(y[:, g, :], y[:, g, :], ACT.Identity, bias=ln_b[:, g:g + 1]).then_inc(v_ready, 1)
                    next_hi(n // 2, n % 2, (q,))
                    if b == 0:
                        for c in (2 * q, 2 * q + 1):
                            act.wait_ge(centred, c + 1)
                            act.wait_ge(sq_used, SQ_LN + c - 1)
                            act.activation(sq[:, c % 2], y[:, 2 * c:2 * c + 2, :], ACT.Square).then_inc(sq_ready, 1)
                    if (b, q) == (1, 2):
                        root()
                    if 0 <= g < CH:
                        act.wait_ge(v_turned, g + 1)
                        if g >= 2:
                            act.wait_ge(mixed, g - 1)
                            act.wait_ge(v_stored[g % 2], 32 * (g // 2))
                        act.activation(vt[:, g % 2, 0:2, :], ps_t[:, 0:2 * P].rearrange("p (a b) -> p a b", a=2),
                                       ACT.Copy).then_inc(v_copied, 1)
                        act.activation(vt[0:NB, g % 2, 2, :], ps_t[0:NB, 2 * P:3 * P], ACT.Copy).then_inc(v_copied, 1)
                        act.wait_ge(v_copied, 2 * g + 2)
                        cols = slice(g * P, g * P + P)
                        act.dma_start(io["new_cmlp_v_prompt"][0, 0, :, cols], vt[:, g % 2, 1, :]).then_inc(v_stored[g % 2], 16)
                        act.dma_start(io["new_cmlp_v_sample"][0, :, 0, cols], vt[0:NB, g % 2, 2, :]
                                      ).then_inc(v_stored[g % 2], 16)
                act.wait_ge(taken, n + 1)
                act.activation(u[:, 2 * b:2 * b + 2, :], u[:, 2 * b:2 * b + 2, :], ACT.Gelu).then_inc(gelu_ready, 1)
                for c in GATED_AT.get(b, ()):
                    act.wait_ge(gated_ready, c + 1)
                    act.activation(ahi[:, 2 * c:2 * c + 2, :], u[:, 2 * c:2 * c + 2, :], ACT.Copy).then_inc(gated_hi, 1)
            product_with_norm(N_COUT, 2)
            for slot in range(2):
                act.wait_ge(v_stored[slot], 32 * CH // 2)
            norm_residual(2)
            ffn(1, N_FFN[1], True)
            root()
            for c in range(4):
                act.wait_ge(y_turned, c + 1)
                for t in (0, 2):
                    rows_ = P if t < 2 else NB
                    act.activation(out_tok[0:rows_, t, 512 * c:512 * c + 512], ps[0:rows_, 3 * (c % 2) + t, :], ACT.Copy
                                   ).then_inc(y_copied_a, 1)

        @block.vector
        def _(dve):
            done = [0]
            stats = [0]

            def step(ins):
                done[0] += 1
                ins.then_inc(chain, 1)
                dve.wait_ge(chain, done[0])

            def w_lo(P2, par, q):
                dve.wait_ge(w_hi_ready, 8 * P2 + 4 * par + q + 1)
                k = slice(QK * (q % 2), QK * (q % 2) + QK)
                dve.tensor_tensor(wlo[:, QK * q:QK * q + QK, :], raw[:, 2 * par + q // 2, k, :],
                                  whi[:, QK * q:QK * q + QK, :].bitcast(F32), ALU.subtract).then_inc(w_lo_ready, 1)

            def next_lo(P2, par, qs):
                for q in qs:
                    w_lo(P2 + par, 1 - par, q)

            def rsqrt(out, st, homogeneous=False):
                dve.wait_ge(stat_ready, st + 1)
                if homogeneous:
                    dve.scalar_tensor_tensor(out=var[:, :], in0=rs_pre[:, :], scalar=EPS, in1=ps_stat, op0=ALU.mult,
                                             op1=ALU.add).then_inc(var_ready, 1)
                else:
                    dve.tensor_scalar(var[:, :], ps_stat, EPS, None, ALU.add).then_inc(var_ready, 1)
                stats[0] += 1
                dve.wait_ge(root_ready, stats[0])
                step(dve.reciprocal(out[:, :], tmp[:, :]))
                step(dve.tensor_tensor(tmp[:, :], out[:, :], out[:, :], ALU.mult))
                step(dve.scalar_tensor_tensor(out=tmp[:, :], in0=tmp[:, :], scalar=-0.5, in1=var[:, :], op0=ALU.mult,
                                              op1=ALU.mult))
                step(dve.scalar_tensor_tensor(out=out[:, :], in0=tmp[:, :], scalar=1.5, in1=out[:, :], op0=ALU.add,
                                              op1=ALU.mult))

            def lo_pair(k, c):
                dve.wait_ge(h_hi_ready, PAIRS * k + c + 1)
                for t in (2 * c, 2 * c + 1):
                    ins = dve.scalar_tensor_tensor(out=hlo[:, t, :], in0=x[:, t, :], scalar=gains[:, G_PRE[k], t:t + 1],
                                                   in1=hhi[:, t, :].bitcast(F32), op0=ALU.mult, op1=ALU.subtract)
                ins.then_inc(h_ready, 1)

            def norm_residual(k, homogeneous):
                rsqrt(rs_post, MIX_POST[k][1], homogeneous)
                for c in range(PAIRS + 2):
                    if c < PAIRS:
                        for t in (2 * c, 2 * c + 1):
                            ins = dve.scalar_tensor_tensor(out=y[:, t, :], in0=y[:, t, :],
                                                           scalar=gains[:, G_POST[k], t:t + 1], in1=rs_post[:, :],
                                                           op0=ALU.mult, op1=ALU.mult)
                        ins.then_inc(scaled, 1)
                        if k == 3 and c % 2:
                            dve.wait_ge(scaled, PAIRS * k + c + 1)
                            dve.tensor_tensor(x[:, 2 * c:2 * c + 2, :], x[:, 2 * c:2 * c + 2, :],
                                              y[:, 2 * c:2 * c + 2, :], ALU.add).then_inc(x_added_v, 1)
                    if k < 3 and c >= 2:
                        lo_pair(k + 1, c - 2)

            dve.wait_ge(g_ready, 1)
            for c in range(PAIRS):
                dve.wait_ge(x_turned, c + 1)
                dve.tensor_copy(x[:, 2 * c:2 * c + 2, :], ps[:, 2 * (c % 3):2 * (c % 3) + 2, 0:T]).then_inc(x_ready, 1)
                if c:
                    lo_pair(0, c - 1)
                if 1 <= c <= NQ:
                    w_lo(0, 0, c - 1)
            lo_pair(0, PAIRS - 1)
            next_lo(0, 0, (0, 1))
            dve.wait_ge(sinks_in, 16)
            dve.wait_ge(state_ready, 1)
            for e in range(2):
                ins = dve.tensor_copy(sink_r[:, 64 * e:64 * e + 64].rearrange("p (b a) -> p b a", b=NB),
                                      sinks[:, :].rearrange("p (a e) -> p e a", e=2)[:, e, :].unsqueeze(1)
                                      .to_broadcast([P, NB, 8]))
            ins.then_inc(sink_ready, 1)
            next_lo(0, 0, (2, 3))
            rsqrt(rs_pre, ST_X0)
            dve.wait_ge(rope_in, 32)
            step(dve.tensor_tensor(cos[:, :], cos[:, :], rs_pre[:, :], ALU.mult))
            step(dve.tensor_tensor(sin[:, :], sin[:, :], rs_pre[:, :], ALU.mult))

            def even_task(n, q):
                if (n, q) == (N_PR, 0):
                    dve.wait_ge(win_scored, NB)
                    dve.tensor_scalar(sc_s.rearrange("p (a b) -> p a b", a=2), ps_s[:, :, 0:64], SCALE, None, ALU.mult
                                      ).then_inc(sc_ready, 1)
                if (n, q) == (2, 0):
                    dve.wait_ge(sink_turned, 1)
                    step(dve.tensor_copy(small[:, 0:1], ps[:, 5, 0:1]))
                if (n, q) == (N_PR, 1):
                    dve.wait_ge(sc_turned, 1)
                    step(dve.tensor_reduce(small[:, 1:2], ps_t[:, 0:P], AX.X, ALU.max))
                    step(dve.tensor_tensor(small[:, 1:2], small[:, 1:2], small[:, 0:1], ALU.max))
                    step(dve.tensor_scalar(small[:, 1:2], small[:, 1:2], -1.0, None, ALU.mult))
                    dve.tensor_tensor(small[:, 2:3], small[:, 0:1], small[:, 1:2], ALU.add).then_inc(s_max, 1)
                if (n, q) == (N_PR, 3):
                    dve.wait_ge(s_exp, 2)
                    step(dve.tensor_tensor(small[:, 5:6], small[:, 3:4], small[:, 4:5], ALU.add))
                    step(dve.reciprocal(small[:, 6:7], small[:, 5:6]))
                    dve.tensor_scalar(p_s[:, :], p_s[:, :], small[:, 6:7], None, ALU.mult).then_inc(s_prob, 1)
                if (n, q) == (N_PR + 2, 0):
                    dve.wait_ge(s_hi, 1)
                    dve.tensor_tensor(alo[:, 0:8, SEQ:], ps_v[:, 0:8 * NB].rearrange("p (a b) -> p a b", a=8),
                                      ahi[:, 0:8, SEQ:].bitcast(F32), ALU.subtract).then_inc(s_attn, 1)
                if q == 2 and N_PR <= n < N_PR + 8:
                    it = n - N_PR
                    g, qi = divmod(it, 2)
                    w = (1 + qi) * P
                    dve.wait_ge(scored, it + 1)
                    if it == 0:
                        dve.wait_ge(mask_ready, 1)
                    for e in range(2):
                        ins = dve.scalar_tensor_tensor(
                            out=S[:, e, :, 0:w], in0=ps_s[:, e, :].rearrange("p (a b) -> p a b", a=2)[:, :, 0:w],
                            scalar=SCALE, in1=mask[:, 2 * P - w:].unsqueeze(1).to_broadcast([P, 2, w]), op0=ALU.mult,
                            op1=ALU.add)
                    step(ins)
                    step(dve.tensor_reduce(small[:, 8:12], S.rearrange("p e a b -> p (e a) b")[:, :, 0:w], AX.X,
                                           ALU.max))
                    sink = sinks[:, GQA * g:GQA * g + GQA].rearrange("p (a e) -> p e a", e=2)
                    m4 = small[:, 8:12].rearrange("p (e a) -> p e a", e=2)
                    step(dve.tensor_tensor(m4, m4, sink, ALU.max))
                    step(dve.tensor_scalar(small[:, 12:16], small[:, 8:12], -1.0, None, ALU.mult))
                    dve.tensor_tensor(small[:, 20:24].rearrange("p (e a) -> p e a", e=2), sink,
                                      small[:, 12:16].rearrange("p (e a) -> p e a", e=2), ALU.add
                                      ).then_inc(masked, 1)
                if q == 3 and N_PR <= n < N_PR + 8:
                    it = n - N_PR
                    dve.wait_ge(p_exp, it + 1)
                    step(dve.tensor_tensor(small[:, 32:36], small[:, 24:28], small[:, 28:32], ALU.add))
                    dve.reciprocal(small[:, 16:20], small[:, 32:36]).then_inc(p_rec, 1)
                if q == 3 and N_PR < n < N_PR + 9:
                    it = n - N_PR - 1
                    g, qi = divmod(it, 2)
                    dve.wait_ge(attn_hi, it + 1)
                    dve.tensor_tensor(alo[:, 2 * g:2 * g + 2, qi * P:qi * P + P],
                                      ps_v[:, 0:2 * P].rearrange("p (a b) -> p a b", a=2),
                                      ahi[:, 2 * g:2 * g + 2, qi * P:qi * P + P].bitcast(F32), ALU.subtract
                                      ).then_inc(attn_ready, 1)

            for n in range(N_EOUT):
                par = n % 2
                for q in range(NQ - 1 if n else 0):
                    next_lo(n // 2, par, (q,))
                    even_task(n, q)
                i, kind = divmod(n - N_CONV, 3)
                dve.wait_ge(w_used, 4 * n + 4)
                if n < N_V:
                    dst = y[:, 2 * n:2 * n + 2, :]
                    dve.wait_ge(swap_ready, n + 1)
                    dve.tensor_tensor(dst, pair(par), twice(cos[:, :]), ALU.mult)
                    step(dve.tensor_tensor(swp[:, :, :], swp[:, :, :], twice(sin[:, :]), ALU.mult))
                    dve.tensor_tensor(dst, dst, swp[:, :, :], ALU.add).then_inc(taken, 1)
                elif n == N_V:
                    dve.tensor_tensor(y[:, 10:12, :], pair(par), twice(rs_pre[:, :]), ALU.mult).then_inc(taken, 1)
                else:
                    if n == N_CONV:
                        dve.wait_ge(kv_turned, 1)
                    if i and kind < 2:
                        dve.wait_ge(z_ready, i)
                    t = 8 + 2 * kind
                    dve.tensor_tensor(y[:, t:t + 2, :], pair(par), twice(rs_pre[:, :]), ALU.mult).then_inc(taken, 1)
                if n:
                    next_lo(n // 2, par, (NQ - 1,))
                    even_task(n, NQ - 1)
                if n >= N_CONV and kind == 2:
                    dve.wait_ge(tap0_ready, i + 1)
                    if i == 0:
                        dve.wait_ge(conv_s_ready, 1)
                    for tap in (1, 2):
                        for t in range(2):
                            ins = dve.scalar_tensor_tensor(
                                out=y[:, 14 + t, 0:SEQ], in0=z[:, t, tap:tap + SEQ],
                                scalar=conv_w[:, tap, 2 * i + t:2 * i + t + 1], in1=y[:, 14 + t, 0:SEQ], op0=ALU.mult,
                                op1=ALU.add)
                        step(ins)
                    for t in range(2):
                        ins = dve.scalar_tensor_tensor(
                            out=y[:, 14 + t, SEQ:], in0=z[:, t, 2 + SEQ:], scalar=conv_w[:, 2, 2 * i + t:2 * i + t + 1],
                            in1=conv_s[:, 2 * i + t, :], op0=ALU.mult, op1=ALU.add)
                    step(ins)
                    dve.tensor_tensor(y[:, 14:16, :], y[:, 14:16, :], y[:, 12:14, :], ALU.mult).then_inc(conv_done, 1)
                    dve.wait_ge(conv_hi, i + 1)
                    dve.tensor_tensor(alo[:, 8 + 2 * i:10 + 2 * i, :], y[:, 14:16, :],
                                      ahi[:, 8 + 2 * i:10 + 2 * i, :].bitcast(F32), ALU.subtract
                                      ).then_inc(conv_ready, 1)

            def product_to_y(n0):
                with dve.Fori(0, UNIT // 2) as i:
                    for par in range(2):
                        n = n0 + 2 * i + par
                        next_lo(n0 // 2 + i, par, (0, 1, 2))
                        dve.wait_ge(w_used, 4 * n + 4)
                        dve.tensor_copy(y[:, bass.ds(4 * i + 2 * par, 2), :], pair(par)).then_inc(taken, 1)
                        next_lo(n0 // 2 + i, par, (3,))

            def add_block(P2, par, i, cut=True):
                if cut:
                    next_lo(P2, par, (0, 1, 2))
                dve.wait_ge(w_used, 8 * P2 + 4 * par + 4)
                dst = y[:, bass.ds(2 * i, 2), :]
                dve.tensor_tensor(dst, dst, pair(par), ALU.add).then_inc(taken, 1)
                if cut:
                    next_lo(P2, par, (3,))

            def up_blocks(P0, m0):
                with dve.Fori(0, UNIT // 2) as i:
                    for par in range(2):
                        m = m0 + 2 * i + par
                        next_lo(P0 + i, par, (0, 1, 2))
                        dve.wait_ge(w_used, 8 * (P0 + i) + 4 * par + 4)
                        dve.tensor_scalar(relu[:, :, :], pair(par), 0.0, None, ALU.max).then_inc(taken, 1)
                        next_lo(P0 + i, par, (3,))
                        dve.wait_ge(asq_ready, 2 * m + 2)
                        dve.tensor_tensor(alo[:, bass.ds(4 * i + 2 * par, 2), :], asq[:, :, :],
                                          ahi[:, bass.ds(4 * i + 2 * par, 2), :].bitcast(F32), ALU.subtract
                                          ).then_inc(a_ready, 1)

            def ffn(l, n0, last):
                dve.wait_ge(y_zero, l + 1)
                P0, m0 = n0 // 2, FG * UNIT * l
                with dve.Fori(0, FG - 1) as j:
                    up_blocks(P0 + UNIT * j, m0 + UNIT * j)
                    with dve.Fori(0, UNIT // 2) as i:
                        for par in range(2):
                            add_block(P0 + UNIT * j + UNIT // 2 + i, par, 2 * i + par)
                P0, m0 = P0 + UNIT * (FG - 1), m0 + UNIT * (FG - 1)
                up_blocks(P0, m0)
                dve.wait_ge(stat_ready, PRE[2 * l + 1][1] + 1)
                step(dve.tensor_scalar(tmp[:, :], ps_stat, EPS, None, ALU.add))
                step(dve.tensor_tensor(rs_pre[:, :], tmp[:, :], tmp[:, :], ALU.mult))
                P0 = P0 + UNIT // 2
                with dve.Fori(0, UNIT // 2 - 1 if last else UNIT // 2) as i:
                    for par in range(2):
                        add_block(P0 + i, par, 2 * i + par)
                if last:
                    add_block(P0 + UNIT // 2 - 1, 0, UNIT - 2)
                    add_block(P0 + UNIT // 2 - 1, 1, UNIT - 1, cut=False)

            product_to_y(N_EOUT)
            norm_residual(0, False)
            ffn(0, N_FFN[0], False)
            norm_residual(1, True)

            def scale_v(n, par, i):
                dve.wait_ge(w_used, 4 * n + 4)
                dve.tensor_tensor(y[:, bass.ds(2 * i, 2), :], pair(par), twice(rs_pre[:, :]), ALU.mult
                                  ).then_inc(taken, 1)

            next_lo(N_CIN // 2, 0, range(NQ))
            rsqrt(rs_pre, ST_PRE2)
            dve.wait_ge(x_added, 2 * PAIRS)
            scale_v(N_CIN, 0, 0)
            next_lo(N_CIN // 2, 1, (0, 1, 2))
            scale_v(N_CIN + 1, 1, 1)
            next_lo(N_CIN // 2, 1, (3,))
            with dve.Fori(1, UNIT // 2) as i:
                for par in range(2):
                    next_lo(N_CIN // 2 + i, par, (0, 1, 2))
                    scale_v(N_CIN + 2 * i + par, par, 2 * i + par)
                    next_lo(N_CIN // 2 + i, par, (3,))
            for b in range(UNIT):
                n = N_CIN + UNIT + b
                par = n % 2
                for q in range(NQ):
                    g = NQ * (b - 2) + q
                    if 0 <= g < CH:
                        dve.scalar_tensor_tensor(out=y[:, g, :], in0=y[:, g, :], scalar=ln_g[:, g:g + 1],
                                                 in1=rs_post[:, :], op0=ALU.mult, op1=ALU.mult).then_inc(ln_scaled, 1)
                    if q == NQ - 1:
                        dve.wait_ge(w_used, 4 * n + 4)
                        dve.tensor_tensor(u[:, 2 * b:2 * b + 2, :], pair(par), twice(rs_pre[:, :]), ALU.mult
                                          ).then_inc(taken, 1)
                    next_lo(n // 2, par, (q,))
                    if b == 0:
                        if q == 0:
                            dve.wait_ge(stat_ready, ST_MEAN + 1)
                            step(dve.tensor_copy(rs_post[:, :], ps_stat))
                        for c in (2 * q, 2 * q + 1):
                            dve.wait_ge(gelu_ready, c + 1)
                            dve.tensor_tensor(y[:, 2 * c:2 * c + 2, :], y[:, 2 * c:2 * c + 2, :],
                                              twice(rs_post[:, :]), ALU.subtract).then_inc(centred, 1)
                    if (b, q) == (1, 2):
                        rsqrt(rs_post, ST_LN)
                    if 0 <= g - 1 < CH:
                        g -= 1
                        dve.wait_ge(mixed, g + 1)
                        if g == 0:
                            dve.wait_ge(bias_in, 16)
                            dve.wait_ge(ws_ready, 3)
                        dve.tensor_scalar(y[:, g, SEQ:], y[:, g, SEQ:], ws00[:, g:g + 1], b_bc[:, g, 0:1], ALU.mult,
                                          ALU.add)
                        dve.tensor_tensor(y[:, g, 0:SEQ].rearrange("p (a b) -> p a b", a=2),
                                          ps_v[:, 0:SEQ].rearrange("p (a b) -> p a b", a=2),
                                          twice(b_bc[:, g, :]), ALU.add).then_inc(mix_ready, 1)
                for c in GATED_AT.get(b, ()):
                    dve.wait_ge(gelu_ready, UNIT + c + 1)
                    dve.wait_ge(mix_ready, 2 * c + 2)
                    dve.tensor_tensor(u[:, 2 * c:2 * c + 2, :], u[:, 2 * c:2 * c + 2, :], y[:, 2 * c:2 * c + 2, :],
                                      ALU.mult).then_inc(gated_ready, 1)
                for c in GATED_AT.get(b, ()):
                    dve.wait_ge(gated_hi, c + 1)
                    dve.tensor_tensor(alo[:, 2 * c:2 * c + 2, :], u[:, 2 * c:2 * c + 2, :],
                                      ahi[:, 2 * c:2 * c + 2, :].bitcast(F32), ALU.subtract).then_inc(g_lo_ready, 1)
            product_to_y(N_COUT)
            norm_residual(2, False)
            ffn(1, N_FFN[1], True)
            norm_residual(3, True)
            for c in range(4):
                dve.wait_ge(y_turned, c + 1)
                dve.tensor_copy(out_tok[:, 1, 512 * c:512 * c + 512], ps[:, 3 * (c % 2) + 1, :]).then_inc(y_copied_v, 1)

        @block.tensor
        def _(pe):
            def quarter(n, par, q, hi, lo, operand=None):
                if q == 0 and not (isinstance(n, int) and n < 2):
                    pe.wait_ge(taken, n - 1)
                pe.wait_ge(w_lo_ready, 4 * n + q + 1)
                for k in range(QK * q, QK * q + QK):
                    if operand:
                        operand(k)
                    for j in range(2):
                        cols = slice(P * j, P * j + P)
                        out = ps[:, 2 * par + j, 0:T]
                        pe.matmul(out, whi[:, k, cols], hi[:, k, :], start=(k == 0), stop=False)
                        pe.matmul(out, whi[:, k, cols], lo[:, k, :], start=False, stop=False)
                        mm = pe.matmul(out, wlo[:, k, cols], hi[:, k, :], start=False, stop=(k == CH - 1))
                mm.then_inc(w_used, 1)

            def h_operand(k_norm):
                def wait(k):
                    if k % 2 == 0:
                        pe.wait_ge(h_ready, PAIRS * k_norm + k // 2 + 1)
                return wait

            def statistic(acc, tail=None):
                for j in range(2):
                    mm = pe.matmul(ps_stat, mean_w[:, :], acc[:, j, :], start=(j == 0), stop=(j == 1 and not tail))
                if tail:
                    tail()
                    for j in range(2):
                        mm = pe.matmul(ps_stat, mean_w[:, :], sq_tail[:, j, :], start=False, stop=(j == 1))
                mm.then_inc(stat_ready, 1)

            pe.wait_ge(const_ready, 2)
            for c in range(PAIRS):
                if c >= 3:
                    pe.wait_ge(x_ready, c - 2)
                for tok in range(3):
                    if c == 0:
                        pe.wait_ge(x_in[tok], 16)
                    for t in range(2):
                        tile, bank = 2 * c + t, 2 * (c % 3) + t
                        cols = slice(P * tile, P * tile + P)
                        if tok < 2:
                            mm = pe.transpose(ps[:, bank, P * tok:P * tok + P], x_tok[:, tok, cols], ident[:, :])
                        else:
                            mm = pe.transpose(ps[:, bank, SEQ:T], x_tok[0:NB, 2, cols], ident[0:NB, 0:NB])
                mm.then_inc(x_turned, 1)
                if c == 0:
                    pe.wait_ge(g_in, 16 * 4)
                    pe.transpose(ps[:, 6, 0:P], g_rows[:, 0, :], ident[:, :]).then_inc(g_turned, 1)
            pe.wait_ge(state_in, 16)
            pe.wait_ge(l_in, 16 * 3)
            n_small = 2 * CH + 3 * CONVT
            pe.transpose(ps[:, 7, 0:n_small], g_rows[0:n_small, 1, :], ident[0:n_small, 0:n_small])
            pe.wait_ge(x_ready, PAIRS)
            for c in range(CONVT):
                mm = pe.transpose(ps[:, 4, 16 * c:16 * c + 16], state_tok[0:2 * NB, P * c:P * c + P],
                                  ident[0:2 * NB, 0:2 * NB])
            mm.then_inc(state_turned, 1)

            def even_task(n, q):
                if (n, q) == (1, 0):
                    pe.wait_ge(sq_used, SQ_X0 + PAIRS)
                    pe.wait_ge(g_ready, 2)
                    statistic(acc_pre)
                if (n, q) == (1, 1):
                    pe.wait_ge(sink_ready, 1)
                    pe.transpose(ps[:, 5, 0:P], sink_r[:, :], ident[:, :]).then_inc(sink_turned, 1)
                if (n, q) == (N_CONV, 1):
                    pe.wait_ge(taken, N_CONV)
                    for kv in range(2):
                        for t in range(QT):
                            for h in range(2):
                                pe.transpose(ps[:, 4 + kv, KVW * t + P * h:KVW * t + P * h + P],
                                             y[:, 8 + 2 * kv + h, P * t:P * t + P], ident[:, :])
                        for h in range(2):
                            mm = pe.transpose(ps[0:NB, 6, KVW * kv + P * h:KVW * kv + P * h + P],
                                              y[:, 8 + 2 * kv + h, SEQ:], ident[:, :])
                    mm.then_inc(kv_turned, 1)
                if (n, q) == (N_CONV, 3):
                    pe.wait_ge(kv_copied, 3)
                    for g in range(NKV):
                        for t in range(QT):
                            col = SEQ * (g % 2) + P * t
                            mm = pe.transpose(ps[:, 4 + g // 2, col:col + P],
                                              k_tok[:, t, HD * g:HD * g + P],
                                              ident[:, :])
                    mm.then_inc(k2_turned, 1)

                def win_scores(b):
                    pe.wait_ge(win_copied, b + 1)
                    if b == 0:
                        pe.wait_ge(k2_ready, 1)
                    for e in range(2):
                        for g in range(NKV):
                            col = 8 * b + 2 * g
                            mm = pe.matmul(ps_s[:, e, col:col + 2], kt_win[HD * e:HD * e + HD, b % 2, (g - e) % NKV, :],
                                           y[HD * e:HD * e + HD, 2 * g:2 * g + 2, SEQ + b], start=True, stop=True)
                    mm.then_inc(win_scored, 1)

                if N_SAMP <= n < N_SAMP + 2:
                    b = NQ * (n - N_SAMP) + q
                    if b == 0:
                        pe.wait_ge(win_ready, 1)
                        pe.wait_ge(kv_copied, 4)
                    else:
                        pe.wait_ge(win_copied, b)
                    for g in range(NKV):
                        mm = pe.transpose(ps_t[:, P * g:P * g + P],
                                          k_win[:, b, HD * g:HD * g + P],
                                          ident[:, :])
                    mm.then_inc(win_turned, 1)
                    if b:
                        win_scores(b - 1)
                if (n, q) == (N_PR, 0):
                    win_scores(NB - 1)
                if (n, q) == (N_PR, 1):
                    pe.wait_ge(sc_ready, 1)
                    pe.transpose(ps_t[:, 0:P], sc_s[:, :], ident[:, :]).then_inc(sc_turned, 1)
                if (n, q) == (N_PR + 1, 0):
                    pe.wait_ge(s_prob, 1)
                    pe.transpose(ps_t[:, 0:P], p_s[:, :], ident[:, :]).then_inc(s_pturned, 1)
                if (n, q) == (N_PR + 2, 0):
                    pe.wait_ge(s_pt, 1)
                    pe.wait_ge(attn_ready, 1)
                    for e in range(2):
                        for b in range(NB):
                            for g in range(NKV):
                                col = 64 * e + 8 * b + 2 * g
                                out = ps_v[HD * e:HD * e + HD, 0:8 * NB].rearrange("p (a b) -> p a b", a=8)
                                mm = pe.matmul(out[:, 2 * g:2 * g + 2, b], v_win[:, b, HD * g:HD * g + HD],
                                               pt_s[:, col:col + 2], start=True, stop=True)
                    mm.then_inc(s_pv, 1)
                if q in (1, 2) and N_PR < n < N_PR + 9:
                    it, kb = n - N_PR - 1, q - 1
                    if kb == 0 or it % 2:
                        count = it // 2 * 3 + (it % 2) + kb
                        if kb == 0:
                            pe.wait_ge(p_norm, it + 1)
                        if count == 0:
                            pe.wait_ge(s_pt, 1)
                        else:
                            pe.wait_ge(p_copied, count)
                        for e in range(2):
                            for jj in range(2):
                                col = P * (2 * e + jj)
                                mm = pe.transpose(ps_t[:, col:col + P], S[:, e, jj, P * kb:P * kb + P], ident[:, :])
                        mm.then_inc(p_turned, 1)
                if q == 3 and N_PR < n < N_PR + 9:
                    it = n - N_PR - 1
                    g, qi = divmod(it, 2)
                    pe.wait_ge(p_copied, it // 2 * 3 + (it % 2) * 2 + 1)
                    if it:
                        pe.wait_ge(attn_ready, it)
                    if it == 1:
                        pe.wait_ge(s_attn, 1)
                    for kb in range(1 + qi):
                        for e in range(2):
                            mm = pe.matmul(ps_v[HD * e:HD * e + HD, 0:2 * P], v_tok[:, kb, HD * g:HD * g + HD],
                                           PT[:, kb, 2 * e:2 * e + 2, :], start=(kb == 0), stop=(kb == qi))
                    mm.then_inc(pv_done, 1)
                if q == 2 and N_PR <= n < N_PR + 8:
                    it = n - N_PR
                    g, qi = divmod(it, 2)
                    w = (1 + qi) * P
                    if it == 0:
                        pe.wait_ge(sc_ready, 1)
                    else:
                        pe.wait_ge(masked, it)
                    for jj in range(2):
                        for e in range(2):
                            rows_ = slice(HD * e, HD * e + HD)
                            mm = pe.matmul(ps_s[:, e, SEQ * jj:SEQ * jj + w], y[rows_, 2 * g + jj, P * qi:P * qi + P],
                                           kt2[rows_, (g - e) % NKV, 0:w], start=True, stop=True)
                    mm.then_inc(scored, 1)

            for n in range(N_EOUT):
                for q in range(NQ):
                    quarter(n, n % 2, q, hhi, hlo, h_operand(0) if n == 0 else None)
                    even_task(n, q)

            def attn_operand(k):
                if k == 0:
                    pe.wait_ge(s_attn, 1)
                if k in (0, 2, 4, 6):
                    pe.wait_ge(attn_ready, k + 2)
                if k >= 8 and k % 2 == 0:
                    pe.wait_ge(conv_ready, (k - 8) // 2 + 1)

            def gated_operand(k):
                if k % 2 == 0:
                    pe.wait_ge(g_lo_ready, k // 2 + 1)

            def product(n0, hi, lo, operand, pairs=UNIT // 2):
                with pe.Fori(0, pairs) as i:
                    for par in range(2):
                        for q in range(NQ):
                            quarter(n0 + 2 * i + par, par, q, hi, lo, operand if par == 0 else None)

            def post_statistic(k):
                pe.wait_ge(sq_used, MIX_POST[k][0] + TAIL)
                statistic(acc_post, lambda: pe.wait_ge(tail_ready, k + 1))

            product(N_EOUT, ahi, alo, attn_operand)
            pe.wait_ge(z_ready, 4)
            pe.wait_ge(masked, 8)
            for c in range(CONVT):
                mm = pe.transpose(ps[0:2 + NB, 4 + c // 4, P * (c % 4):P * (c % 4) + P], z_last[:, c, :], ident[:, :])
            mm.then_inc(z_turned, 1)
            pe.wait_ge(attn_ready, 8)
            post_statistic(0)

            def turn_ws(r):
                if r == 0:
                    pe.wait_ge(ws_masked, 1)
                    pe.wait_ge(z_out, 1)
                else:
                    pe.wait_ge(ws_ready, r)
                for g in range(8):
                    mm = pe.transpose(ps_s[:, g // 4, P * (g % 4):P * (g % 4) + P], ws_raw[:, 8 * r + g, :], ident[:, :])
                if r:
                    mm = pe.matmul(ps[:, 6, 0:CH], mean_w[0:1, :], ws_raw[0:1, :, 0], start=True, stop=True)
                mm.then_inc(ws_turned, 1)

            def ffn(l, n0):
                def up(base, m0):
                    def hidden(k):
                        if k % 2 == 0:
                            pe.wait_ge(a_ready, m0 + k // 2 + 1)
                    product(base, hhi, hlo, h_operand(2 * l + 1))
                    return hidden

                with pe.Fori(0, FG - 1) as j:
                    base = n0 + 2 * UNIT * j
                    hidden = up(base, FG * UNIT * l + UNIT * j)
                    product(base + UNIT, ahi, alo, hidden)
                if l == 0:
                    turn_ws(0)
                base = n0 + 2 * UNIT * (FG - 1)
                hidden = up(base, FG * UNIT * l + UNIT * (FG - 1))
                if l == 0:
                    turn_ws(1)
                pe.wait_ge(sq_used, PRE[2 * l + 1][0] + PAIRS)
                statistic(acc_pre)
                product(base + UNIT, ahi, alo, hidden)
                post_statistic(2 * l + 1)

            ffn(0, N_FFN[0])
            for par in range(2):
                for q in range(NQ):
                    quarter(N_CIN + par, par, q, hhi, hlo, h_operand(2))
                    if (par, q) == (1, 1):
                        pe.wait_ge(sq_used, PRE[2][0] + PAIRS)
                        statistic(acc_pre)
            product(N_CIN + 2, hhi, hlo, None, UNIT // 2 - 1)

            def v_tokens(g):
                pe.wait_ge(v_ready, g + 1)
                if g:
                    pe.wait_ge(v_copied, 2 * g)
                pe.transpose(ps_t[:, 0:P], y[:, g, 0:P], ident[:, :])
                pe.transpose(ps_t[:, P:2 * P], y[:, g, P:2 * P], ident[:, :])
                pe.transpose(ps_t[0:NB, 2 * P:3 * P], y[:, g, SEQ:], ident[:, :]).then_inc(v_turned, 1)

            def mix(g):
                pe.wait_ge(v_copied, 2 * g + 2)
                if g == 0:
                    pe.wait_ge(ws_ready, 2)
                    pe.wait_ge(ln_scaled, 1)
                else:
                    pe.wait_ge(mix_ready, g)
                for c in range(QT):
                    mm = pe.matmul(ps_v[:, P * c:P * c + P], vt[:, g % 2, c, :], ws_t[:, g, :], start=True, stop=True)
                mm.then_inc(mixed, 1)

            for b in range(UNIT):
                n = N_CIN + UNIT + b
                for q in range(NQ):
                    quarter(n, n % 2, q, hhi, hlo)
                    if (b, q) == (0, 0):
                        pe.wait_ge(v_summed, PAIRS)
                        statistic(acc_post)
                    if (b, q) == (1, 2):
                        pe.wait_ge(sq_used, SQ_LN + PAIRS)
                        statistic(acc_pre)
                    if 2 <= b <= 5:
                        g = 4 * (b - 2) + q
                        if g:
                            mix(g - 1)
                        v_tokens(g)
                    if (b, q) == (6, 0):
                        mix(CH - 1)
            product(N_COUT, ahi, alo, gated_operand)
            post_statistic(2)
            ffn(1, N_FFN[1])
            for c in range(4):
                pe.wait_ge(x_added, 3 * PAIRS + c + 1)
                pe.wait_ge(x_added_v, c + 1)
                if c >= 2:
                    pe.wait_ge(y_copied_a, 2 * c - 2)
                    pe.wait_ge(y_copied_v, c - 1)
                for t in range(3):
                    rows_, toks = (P, slice(P * t, P * t + P)) if t < 2 else (NB, slice(SEQ, T))
                    for k in range(4):
                        mm = pe.transpose(ps[0:rows_, 3 * (c % 2) + t, P * k:P * k + P], x[:, 4 * c + k, toks],
                                          ident[:, :])
                mm.then_inc(y_turned, 1)


def rope_tables():
    half = HD // 2
    inv_freq = (10000.0 ** (-np.arange(half) / half)).astype(np.float32)
    pos = np.concatenate([np.arange(SEQ), np.full(NB, 2048)]).astype(np.float32)
    ang = (pos[None, :] * inv_freq[:, None]).astype(np.float32).astype(np.float64)
    c, s = np.cos(ang), np.sin(ang)
    return (np.concatenate([c, c, c, c]).astype(np.float32),
            np.concatenate([-s, s, -s, s]).astype(np.float32))


_INS = ['x_prompt', 'x_sample', 'cache_k_win', 'cache_v_win', 'state_conv', 'w_in_even', 'w_out_even', 'conv_w',
        'attn_sinks', 'w_in_cmlp', 'w_out_cmlp', 'ln_v_g', 'ln_v_b', 'w_spatial', 'b_spatial', 'w_ffn_up',
        'w_ffn_down', 'g_mix_pre', 'g_mix_post', 'g_ffn_pre', 'g_ffn_post']
_OUTS = [('y_prompt', (1, SEQ, D)), ('y_sample', (NB, 1, D)), ('new_k_win_prompt', (1, 1, WIN, NKV, HD)),
         ('new_v_win_prompt', (1, 1, WIN, NKV, HD)), ('new_conv_prompt', (1, 1, 2, CONV)),
         ('new_cmlp_v_prompt', (1, 1, P, D)), ('new_k_win_sample', (1, NB, WIN, NKV, HD)),
         ('new_v_win_sample', (1, NB, WIN, NKV, HD)), ('new_conv_sample', (1, NB, 2, CONV)),
         ('new_cmlp_v_sample', (1, NB, 1, D))]


def kernel(**inputs):
    import concourse.bacc as _bacc
    from concourse.bass_utils import run_bass_kernel_spmd as _run

    nc = _bacc.Bacc("TRN2", target_bir_lowering=False, num_devices=1, dynamic_dma_scratch_size=1024)
    arrays, io = {}, {}
    named = {name: np.ascontiguousarray(inputs[name]) for name in _INS}
    named["rope_cos"], named["rope_sin"] = rope_tables()
    for name, a in named.items():
        arrays[f"in_{name}_dram"] = a
        io[name] = nc.dram_tensor(f"in_{name}_dram", a.shape, mybir.dt.from_np(a.dtype), kind="ExternalInput").ap()
    for name, shape in _OUTS:
        io[name] = nc.dram_tensor(f"out_{name}_dram", shape, F32, kind="ExternalOutput").ap()
    build(nc, io)
    r = _run(nc, [arrays], core_ids=[0])
    return tuple(r.results[0][f"out_{name}_dram"] for name, _ in _OUTS)
```

```python
from contextlib import ExitStack

import numpy as np

import concourse.bass as bass
from concourse import mybir

F32 = mybir.dt.float32
F32R = mybir.dt.float32r
ALU = mybir.AluOpType
ACT = mybir.ActivationFunctionType
AX = mybir.AxisListType

P = 128
D = 2048
CH = D // P
PAIRS = CH // 2
SEQ = 256
NB = 8
T = SEQ + NB
QT = SEQ // P
HD = 64
NH = 16
NKV = 4
GQA = NH // NKV
KVW = NKV * HD
CONV = 1024
CONVT = CONV // P
WIN = 128
FFN = 4 * D
FG = FFN // D
EPS = 1e-6
SCALE = HD ** -0.5
MASKED = -1e30

BC = 256
NQ = 4
QK = CH // NQ
UNIT = D // BC

N_EVEN = 0
N_EOUT = (NH * HD + 2 * KVW + 3 * CONV) // BC
N_FFN = [N_EOUT + UNIT, N_EOUT + UNIT + 2 * UNIT * FG + 3 * UNIT]
N_CIN = N_FFN[0] + 2 * UNIT * FG
N_COUT = N_CIN + 2 * UNIT
N_END = N_FFN[1] + 2 * UNIT * FG

N_K = NH * HD // BC
N_V = N_K + 1
N_CONV = N_V + 1
N_SAMP = N_CONV + 1
N_PR = N_SAMP + 2


def conv_col(n):
    i, part = divmod(n - N_CONV, 3)
    return N_CONV + (4, 8, 0)[part] + i


def even_col(n):
    return n if n < N_CONV else conv_col(n)


def build(nc, io):
    ctx = ExitStack()
    with ctx:
        def sb(name, shape, dt=F32):
            return ctx.enter_context(nc.sbuf_tensor(name, shape, dt))

        def sem(name):
            return ctx.enter_context(nc.semaphore(name))

        raw = sb("raw", [P, 4, 2 * QK, BC])
        whi = sb("whi", [P, CH, BC], F32R)
        wlo = sb("wlo", [P, CH, BC], F32R)
        x = sb("x", [P, CH, T])
        y = sb("y", [P, CH, T])
        hhi = sb("hhi", [P, CH, T], F32R)
        hlo = sb("hlo", [P, CH, T], F32R)
        ahi = sb("ahi", [P, CH, T], F32R)
        alo = sb("alo", [P, CH, T], F32R)
        ident = sb("ident", [P, P])
        mean_w = sb("mean_w", [P, P])
        cos = sb("cos", [P, T])
        sin = sb("sin", [P, T])
        rs_pre = sb("rs_pre", [P, T])
        rs_post = sb("rs_post", [P, T])
        var = sb("var", [P, T])
        tmp = sb("tmp", [P, T])
        acc_pre = sb("acc_pre", [P, 2, T])
        acc_post = sb("acc_post", [P, 2, T])
        sq = sb("sq", [P, 2, 2, T])
        sq_tail = sb("sq_tail", [P, 2, T])
        gains = sb("gains", [P, 8, CH])
        lnw = sb("lnw", [P, 2 * CH + 3 * CONVT])
        sinks = sb("sinks", [P, NH])
        small = sb("small", [P, 48])
        ln_g = lnw[:, 0:CH]
        ln_b = lnw[:, CH:2 * CH]
        conv_w = lnw[:, 2 * CH:].rearrange("p (w c) -> p w c", w=3)

        REGION = 10496
        region = sb("region", [P, REGION])

        def part(start, *dims):
            size = int(np.prod(dims))
            assert start + size <= REGION
            ap = region[:, start:start + size]
            names = "abc"[:len(dims)]
            if len(dims) == 1:
                return ap
            return ap.rearrange(f"p ({' '.join(names)}) -> p {' '.join(names)}", **dict(zip(names, dims)))

        x_tok = part(0, 3, D)
        g_rows = part(3 * D, 2, P)
        state_tok = part(3 * D + 2 * P, CONV)
        S = part(0, 2, 2, 2 * P)
        kt_win = part(0, 2, NKV, P)
        PT = part(1024, 2, 4, P)
        kv_new = part(1024, 2, KVW)
        kt2 = part(2048, NKV, SEQ)
        swp = part(2048, 2, T)
        KROW = KVW + HD
        k_tok = part(3072, QT, KROW)
        v_tok = part(3712, QT, KVW)
        k_win = part(4224, NB, KROW)
        v_win = part(6784, NB, KVW)
        sc_s = part(8832, P)
        attn_s = sc_s.rearrange("p (a b) -> p a b", a=P // NB)[:, 0:8, :]
        q_samp = part(1024 + 2 * KVW, 2, 8, NB)
        p_s = part(8960, P)
        pt_s = part(9088, P)
        sink_r = part(9216, P)
        z = part(9344, 2, T + 2)
        z_last = part(9876, CONVT, 2 + NB)
        state_t = part(9956, CONVT, NB, 2)
        conv_s = part(10084, CONVT, NB)
        mask = part(10148, 2 * P)
        conv_t = part(10404, CONVT, NB)
        z_tok = part(0, CONV)
        u = part(0, CH, T)
        ws_raw = part(0, CH, P)
        ws_t = part(4224, CH, P)
        b_bc = part(4224 + 2048, CH, P)
        ws00 = part(4224 + 4096, CH)
        vt = part(4224 + 4096 + CH, 2, 3, P)
        relu = part(9000, 2, T)
        asq = part(9528, 2, T)
        out_tok = part(0, 3, D)
        y_tok = raw[:, 0].rearrange("p a b -> p (a b)")
        TOK = (0, P, T - P)
        CHUNK = 4 * P
        Y_BANK = (4, 5, 6, 0, 1, 2, 3, 4, 5, 6, 0, 1)
        pre_tok, var_tok, sum_tok, root_tok, sq_tok, corr_tok, factor_tok = (
            small[:, 3 * i:3 * i + 3] for i in range(7))

        ps = ctx.enter_context(nc.psum_tensor("ps", [P, 8, 512], F32))

        def pair(par):
            return ps[:, 2 * par:2 * par + 2, 0:T]

        ps_s = ps[:, 4:6, :]
        ps_t = ps[:, 6, :]
        ps_v = ps[:, 7, :]
        ps_stat = ps[:, 7, 0:T]

        raw_loaded = [sem(f"raw_loaded{i}") for i in range(4)]
        w_hi_ready = sem("w_hi_ready")
        w_lo_ready = sem("w_lo_ready")
        w_used = sem("w_used")
        taken = sem("taken")
        x_in = [sem(f"x_in{i}") for i in range(5)]
        g_in = sem("g_in")
        l_in = sem("l_in")
        sinks_in = sem("sinks_in")
        rope_in = sem("rope_in")
        state_in = sem("state_in")
        win_in = sem("win_in")
        new_in = sem("new_in")
        win_ready = sem("win_ready")
        ws_in = sem("ws_in")
        bias_in = sem("bias_in")
        const_ready = sem("const_ready")
        g_turned = sem("g_turned")
        g_ready = sem("g_ready")
        x_turned = sem("x_turned")
        x_ready = sem("x_ready")
        h_hi_ready = sem("h_hi_ready")
        h_ready = sem("h_ready")
        h_hi_first = sem("h_hi_first")
        h_first = sem("h_first")
        sq_ready = sem("sq_ready")
        sq_used = sem("sq_used")
        tail_taken = sem("tail_taken")
        tail_ready = sem("tail_ready")
        stat_ready = sem("stat_ready")
        var_ready = sem("var_ready")
        root_ready = sem("root_ready")
        scaled = sem("scaled")
        post_ready = sem("post_ready")
        gained = sem("gained")
        x_added = sem("x_added")
        x_added_v = sem("x_added_v")
        y_zero = sem("y_zero")
        chain = sem("chain")
        pool_chain = sem("pool_chain")
        asq_ready = sem("asq_ready")
        a_ready = sem("a_ready")
        swap_ready = sem("swap_ready")
        kv_turned = sem("kv_turned")
        kv_copied = sem("kv_copied")
        k2_turned = sem("k2_turned")
        k2_ready = sem("k2_ready")
        win_turned = sem("win_turned")
        win_copied = sem("win_copied")
        win_scored = sem("win_scored")
        sc_ready = sem("sc_ready")
        sc_turned = sem("sc_turned")
        s_max = sem("s_max")
        s_exp = sem("s_exp")
        s_prob = sem("s_prob")
        s_pturned = sem("s_pturned")
        s_pt = sem("s_pt")
        s_pv = sem("s_pv")
        s_hi = sem("s_hi")
        s_attn = sem("s_attn")
        s_moved = sem("s_moved")
        q_zeroed = sem("q_zeroed")
        q_samp_ready = sem("q_samp_ready")
        scored = sem("scored")
        masked = sem("masked")
        p_exp = sem("p_exp")
        p_rec = sem("p_rec")
        p_norm = sem("p_norm")
        p_turned = sem("p_turned")
        p_copied = sem("p_copied")
        pv_done = sem("pv_done")
        attn_hi = sem("attn_hi")
        attn_ready = sem("attn_ready")
        mask_ready = sem("mask_ready")
        state_turned = sem("state_turned")
        state_ready = sem("state_ready")
        conv_s_ready = sem("conv_s_ready")
        z_ready = sem("z_ready")
        tap0_ready = sem("tap0_ready")
        conv_done = sem("conv_done")
        conv_hi = sem("conv_hi")
        conv_ready = sem("conv_ready")
        z_turned = sem("z_turned")
        z_out = sem("z_out")
        sink_ready = sem("sink_ready")
        sink_turned = sem("sink_turned")
        ws_masked = sem("ws_masked")
        ws_turned = sem("ws_turned")
        ws_ready = sem("ws_ready")
        gelu_ready = sem("gelu_ready")
        v_scaled = sem("v_scaled")
        v_summed = sem("v_summed")
        centred = sem("centred")
        ln_scaled = sem("ln_scaled")
        v_ready = sem("v_ready")
        v_turned = sem("v_turned")
        v_copied = sem("v_copied")
        v_stored = [sem(f"v_stored{i}") for i in range(2)]
        mixed = sem("mixed")
        mix_ready = sem("mix_ready")
        gated_ready = sem("gated_ready")
        gated_hi = sem("gated_hi")
        g_lo_ready = sem("g_lo_ready")
        y_turned = sem("y_turned")
        xt_turned = sem("xt_turned")
        xt_copied = sem("xt_copied")
        factor_ready = sem("factor_ready")
        y_scaled = sem("y_scaled")
        out_ready_v = sem("out_ready_v")
        out_ready_p = sem("out_ready_p")
        stored = sem("stored")
        kv_stored = sem("kv_stored")

        block = ctx.enter_context(nc.Block())

        def twice(ap):
            return ap.unsqueeze(1).to_broadcast([P, 2, ap.shape[-1]])

        def rows(w):
            return w.rearrange("(k p) n -> p k n", p=P)

        w_even = rows(io["w_in_even"][0])
        w_eout = rows(io["w_out_even"][0])
        w_cin = rows(io["w_in_cmlp"][0])
        w_cout = rows(io["w_out_cmlp"][0])
        w_up = [rows(io["w_ffn_up"][l]) for l in range(2)]
        w_down = [rows(io["w_ffn_down"][l]) for l in range(2)]

        SQ_X0, SQ_POST0, SQ_PRE1, SQ_POST1, SQ_PRE2, SQ_LN, SQ_POST2, SQ_PRE3, SQ_POST3 = (
            0, 8, 15, 23, 30, 38, 46, 53, 61)
        TAIL = PAIRS - 1
        ST_X0, ST_POST0, ST_PRE1, ST_POST1, ST_PRE2, ST_MEAN, ST_LN, ST_POST2, ST_PRE3, ST_POST3 = range(10)
        MIX_POST = {0: (SQ_POST0, ST_POST0), 1: (SQ_POST1, ST_POST1), 2: (SQ_POST2, ST_POST2), 3: (SQ_POST3, ST_POST3)}
        PRE = {0: (SQ_X0, ST_X0), 1: (SQ_PRE1, ST_PRE1), 2: (SQ_PRE2, ST_PRE2), 3: (SQ_PRE3, ST_PRE3)}
        G_PRE = {0: 0, 1: 4, 2: 1, 3: 5}
        G_POST = {0: 2, 1: 6, 2: 3, 3: 7}
        def wait_added(engine, k, c):
            if c == 0:
                engine.wait_ge(x_added_v, 2 * k + 2)
            else:
                engine.wait_ge(x_added, (PAIRS - 1) * k + c)

        def norm_bufs(acc):
            return var[:, :], tmp[:, :], acc[:, 0, :], acc[:, 1, :]

        GATE_AT = {(3, 1): 0, (3, 3): 1, (4, 1): 2, (4, 3): 3, (5, 1): 4, (6, 1): 5, (7, 1): 6}
        CUT_AT = {(3, 2): 0, (4, 0): 1, (4, 2): 2, (5, 0): 3, (5, 2): 4, (6, 2): 5, (7, 2): 6}

        def group_at(b, q):
            return NQ * b + q - 2 * NQ - 2

        @block.sync
        def _(sp):
            def load(w, k0, c0, P2, par, halves=(0, 1)):
                for h in halves:
                    if not (isinstance(P2, int) and P2 == 0):
                        sp.wait_ge(w_lo_ready, 8 * P2 + 4 * par - 8 + 2 * h + 2)
                    sp.dma_start(raw[:, 2 * par + h], w[:, bass.ds(k0 + 2 * QK * h, 2 * QK), bass.ds(c0, BC)]
                                 ).then_inc(raw_loaded[2 * par + h], 16)

            def load_x(half):
                cols = slice(D // 2 * half, D // 2 * half + D // 2)
                for t in range(QT):
                    sp.dma_start(x_tok[:, t, cols], io["x_prompt"][0, t * P:(t + 1) * P, cols]
                                 ).then_inc(x_in[2 * half + t], 16)

            load_x(0)
            sp.dma_start(x_tok[0:NB, 2, :], io["x_sample"][:, 0, :]).then_inc(x_in[4], 16)
            load(w_even, 0, BC * even_col(0), 0, 0, (0,))
            load_x(1)
            for n in range(N_EOUT):
                load(w_even, 0, BC * even_col(n), n // 2, n % 2, (0, 1) if n else (1,))
                if n == 0:
                    sp.dma_start(g_rows[0:CH, 1, :], io["ln_v_g"].rearrange("l (c p) -> (l c) p", p=P)
                                 ).then_inc(l_in, 16)
                    sp.dma_start(g_rows[CH:2 * CH, 1, :], io["ln_v_b"].rearrange("l (c p) -> (l c) p", p=P)
                                 ).then_inc(l_in, 16)
                    sp.dma_start(g_rows[2 * CH:2 * CH + 3 * CONVT, 1, :],
                                 io["conv_w"][0].rearrange("w (c p) -> (w c) p", p=P)).then_inc(l_in, 16)
                if n == 1:
                    sp.dma_start(cos[:, :], io["rope_cos"]).then_inc(rope_in, 16)
                    sp.dma_start(sin[:, :], io["rope_sin"]).then_inc(rope_in, 16)
                if n == N_K:
                    sp.wait_ge(x_ready, PAIRS)
                    sp.wait_ge(state_ready, 1)
                    for win, cache in ((k_win, io["cache_k_win"]), (v_win, io["cache_v_win"])):
                        for lo, hi in ((0, 112), (112, P - 1)):
                            sp.dma_start(win[lo:hi, :, 0:KVW], cache[0, :, 1 + lo:1 + hi].rearrange("b s g d -> s b (g d)")
                                         ).then_inc(win_in, 16)
            with sp.Fori(0, UNIT // 2) as i:
                for par in range(2):
                    load(w_eout, 0, 2 * BC * i + BC * par, N_EOUT // 2 + i, par)

            def ffn(l, n0):
                with sp.Fori(0, FG) as j:
                    with sp.Fori(0, UNIT // 2) as i:
                        for par in range(2):
                            load(w_up[l], 0, D * j + 2 * BC * i + BC * par, n0 // 2 + UNIT * j + i, par)
                    with sp.Fori(0, UNIT // 2) as i:
                        for par in range(2):
                            load(w_down[l], CH * j, 2 * BC * i + BC * par, n0 // 2 + UNIT // 2 + UNIT * j + i, par)

            ffn(0, N_FFN[0])
            for half in range(2):
                with sp.Fori(0, UNIT // 2) as i:
                    for par in range(2):
                        load(w_cin, 0, D * (1 - half) + 2 * BC * i + BC * par, (N_CIN + UNIT * half) // 2 + i, par)
            with sp.Fori(0, UNIT // 2) as i:
                for par in range(2):
                    load(w_cout, 0, 2 * BC * i + BC * par, N_COUT // 2 + i, par)
            ffn(1, N_FFN[1])
            for c in range(4):
                cols = slice(CHUNK * c, CHUNK * c + CHUNK)
                for t in range(QT):
                    sp.wait_ge(out_ready_v, QT * c + t + 1)
                    sp.dma_start(io["y_prompt"][0, t * P:(t + 1) * P, cols], out_tok[:, t, cols]).then_inc(stored, 16)
                if c < 3:
                    sp.wait_ge(out_ready_p, c + 1)
                else:
                    sp.wait_ge(out_ready_v, QT * 4 + 1)
                sp.dma_start(io["y_sample"][:, 0, cols], out_tok[P - NB:, 2, cols]).then_inc(stored, 16)
            sp.wait_ge(stored, 16 * 12)

        @block.gpsimd
        def _(pool):
            done = [0]

            def step(ins):
                done[0] += 1
                ins.then_inc(pool_chain, 1)
                pool.wait_ge(pool_chain, done[0])

            step(pool.memset(ident[:, :], 0.0))
            pool.affine_select(out=ident[:, :], in_=ident[:, :], compare_op=ALU.not_equal, fill=1.0, base=0,
                               pattern=[[-1, P]], channel_multiplier=1).then_inc(const_ready, 1)
            pool.memset(mean_w[:, :], 1.0 / D).then_inc(const_ready, 1)

            def sum_squares(acc, s0, count=PAIRS, after=None):
                for s in range(s0, s0 + count):
                    pool.wait_ge(sq_ready, s + 1)
                    if s == s0:
                        pool.tensor_copy(acc[:, :, :], sq[:, s % 2]).then_inc(sq_used, 1)
                    else:
                        pool.wait_ge(sq_used, s)
                        pool.tensor_tensor(acc[:, :, :], acc[:, :, :], sq[:, s % 2], ALU.add).then_inc(sq_used, 1)
                    if after:
                        after(s - s0)

            def residual(k):
                def gain(c):
                    g = gains[:, G_POST[k], 2 * c:2 * c + 2].unsqueeze(2).to_broadcast([P, 2, T])
                    pool.tensor_tensor(y[:, 2 * c:2 * c + 2, :], y[:, 2 * c:2 * c + 2, :], g, ALU.mult
                                       ).then_inc(gained, 1)

                sum_squares(acc_post, MIX_POST[k][0], TAIL, gain)
                pool.wait_ge(tail_ready, 2 * k + 2)
                gain(TAIL)
                for c in range(1, PAIRS if k < 3 else 0):
                    if c == 1:
                        pool.wait_ge(post_ready, k + 1)
                        pool.wait_ge(gained, PAIRS * k + 2)
                        step(pool.tensor_tensor(y[:, 2:4, :], y[:, 2:4, :], twice(rs_post[:, :]), ALU.mult))
                    else:
                        pool.wait_ge(scaled, (PAIRS - 2) * k + c - 1)
                    pool.tensor_tensor(x[:, 2 * c:2 * c + 2, :], x[:, 2 * c:2 * c + 2, :], y[:, 2 * c:2 * c + 2, :],
                                       ALU.add).then_inc(x_added, 1)
                if k in (0, 2):
                    wait_added(pool, k, 0)
                    wait_added(pool, k, PAIRS - 1)
                    pool.memset(y[:, :, :], 0.0).then_inc(y_zero, 1)

            sum_squares(acc_pre, SQ_X0)
            pool.wait_ge(x_ready, PAIRS)
            pool.wait_ge(state_ready, 1)
            step(pool.memset(mask[:, :], 0.0))
            step(pool.affine_select(out=mask[:, 0:P], in_=mask[:, 0:P], compare_op=ALU.is_gt, fill=MASKED, base=0,
                                    pattern=[[1, P]], channel_multiplier=-1))
            pool.affine_select(out=mask[:, P:2 * P], in_=mask[:, P:2 * P], compare_op=ALU.is_ge, fill=MASKED,
                               base=0, pattern=[[-1, P]], channel_multiplier=1).then_inc(mask_ready, 1)
            step(pool.memset(z[:, :, 0:2], 0.0))
            for tap in range(2):
                w = conv_w[:, tap, :].unsqueeze(2).to_broadcast([P, CONVT, NB])
                step(pool.tensor_tensor((conv_s if tap == 0 else conv_t)[:, :, :], state_t[:, :, :, tap], w, ALU.mult))
            pool.tensor_tensor(conv_s[:, :, :], conv_s[:, :, :], conv_t[:, :, :], ALU.add).then_inc(conv_s_ready, 1)
            pool.memset(q_samp[:, :, :, :], 0.0).then_inc(q_zeroed, 1)
            pool.wait_ge(new_in, 32)
            pool.tensor_copy(k_win[:, :, KVW:], k_win[:, :, 0:HD]).then_inc(win_ready, 1)
            for n in range(N_CONV, N_EOUT):
                if N_PR <= n < N_PR + 8:
                    it = n - N_PR
                    w = (1 + it % 2) * P
                    pool.wait_ge(p_rec, it + 1)
                    rec = small[:, 16:20].rearrange("p (a b) -> p a b", a=2)
                    for e in range(2):
                        ins = pool.tensor_tensor(S[:, e, :, 0:w], S[:, e, :, 0:w],
                                                 rec[:, e, :].unsqueeze(2).to_broadcast([P, 2, w]), ALU.mult)
                    ins.then_inc(p_norm, 1)
                i, kind = divmod(n - N_CONV, 3)
                if kind == 1:
                    pool.wait_ge(taken, n + 1)
                    if i:
                        pool.wait_ge(conv_done, i)
                    step(pool.tensor_tensor(z[:, :, 2:], y[:, 8:10, :], y[:, 10:12, :], ALU.mult))
                    pool.tensor_copy(z_last[:, 2 * i:2 * i + 2, :], z[:, :, SEQ:]).then_inc(z_ready, 1)
            residual(0)
            pool.wait_ge(ws_in, 16)
            pool.affine_select(out=ws_raw[:, :, :], in_=ws_raw[:, :, :], compare_op=ALU.is_ge, fill=0.0, base=0,
                               pattern=[[0, CH], [-1, P]], channel_multiplier=1).then_inc(ws_masked, 1)
            sum_squares(acc_pre, SQ_PRE1)
            residual(1)
            sum_squares(acc_pre, SQ_PRE2)
            for c in range(PAIRS):
                pool.wait_ge(gelu_ready, c + 1)
                src = y[:, 2 * c:2 * c + 2, :]
                if c == 0:
                    pool.tensor_copy(acc_post[:, :, :], src).then_inc(v_summed, 1)
                else:
                    pool.wait_ge(v_summed, c)
                    pool.tensor_tensor(acc_post[:, :, :], acc_post[:, :, :], src, ALU.add).then_inc(v_summed, 1)
            sum_squares(acc_pre, SQ_LN)
            residual(2)
            sum_squares(acc_pre, SQ_PRE3)
            residual(3)
            pool.wait_ge(xt_copied, 12)
            for c in range(3):
                cols = slice(CHUNK * c, CHUNK * c + CHUNK)
                pool.wait_ge(y_scaled, c + 1)
                pool.tensor_tensor(out_tok[:, 2, cols], out_tok[:, 2, cols], y_tok[:, cols], ALU.add
                                   ).then_inc(out_ready_p, 1)

        @block.scalar
        def _(act):
            roots = [0]

            def root(v, s, w):
                roots[0] += 1
                act.wait_ge(var_ready, roots[0])
                act.activation(s, v, ACT.Sqrt).then_inc(root_ready, 1)
                act.wait_ge(root_ready, 2 * roots[0] - 1)
                act.activation(w, s, ACT.Square).then_inc(root_ready, 1)

            def w_hi(P2, par, q):
                first = isinstance(P2, int) and P2 == 0 and par == 0
                if q % 2 == 0:
                    act.wait_ge(raw_loaded[2 * par + q // 2], 16 * P2 + 16)
                if not first:
                    act.wait_ge(w_used, 8 * P2 + 4 * par - 4 + q + 1)
                k = slice(QK * (q % 2), QK * (q % 2) + QK)
                act.activation(whi[:, QK * q:QK * q + QK, :], raw[:, 2 * par + q // 2, k, :], ACT.Copy
                               ).then_inc(w_hi_ready, 1)

            def next_hi(P2, par, qs=range(NQ)):
                for q in qs:
                    w_hi(P2 + par, 1 - par, q)

            def square_y(n, par, k, i):
                s = MIX_POST[k][0] + i
                if isinstance(i, int) and i == TAIL:
                    act.wait_ge(tail_taken, k + 1)
                    act.activation(sq_tail[:, 0, :], y[:, 2 * i, :], ACT.Square).then_inc(tail_ready, 1)
                    act.wait_ge(taken, n + 1)
                    act.activation(sq_tail[:, 1, :], y[:, 2 * i + 1, :], ACT.Square).then_inc(tail_ready, 1)
                    return
                act.wait_ge(taken, n + 1)
                act.wait_ge(sq_used, s - 1)
                act.activation(sq[:, (MIX_POST[k][0] + par) % 2], y[:, bass.ds(2 * i, 2), :], ACT.Square
                               ).then_inc(sq_ready, 1)

            def hi_pair(k, c):
                for t in (2 * c, 2 * c + 1):
                    if k and t < 2:
                        act.wait_ge(x_added_v, 2 * (k - 1) + t + 1)
                    ins = act.activation(hhi[:, t, :], x[:, t, :], ACT.Copy, scale=gains[:, G_PRE[k], t:t + 1])
                    if t == 0:
                        ins.then_inc(h_hi_first, 1)
                ins.then_inc(h_hi_ready, 1)

            def square_x(k, c):
                s = PRE[k][0] + c
                if s >= 2:
                    act.wait_ge(sq_used, s - 1)
                act.activation(sq[:, s % 2], x[:, 2 * c:2 * c + 2, :], ACT.Square).then_inc(sq_ready, 1)

            def norm_residual(k):
                for c in range(PAIRS):
                    if c:
                        wait_added(act, k, c)
                    hi_pair(k + 1, c)

            for n, name in enumerate(["g_mix_pre", "g_mix_post", "g_ffn_pre", "g_ffn_post"]):
                act.dma_start(g_rows[32 * n:32 * n + 32, 0, :],
                              io[name].rearrange("l (c p) -> (l c) p", p=P)).then_inc(g_in, 16)
            act.dma_start(state_tok[0:2 * NB, :], io["state_conv"][0].rearrange("b r n -> (b r) n")
                          ).then_inc(state_in, 16)
            act.dma_start(sinks[:, :], io["attn_sinks"][0].partition_broadcast(P)).then_inc(sinks_in, 16)

            act.wait_ge(g_turned, 1)
            act.activation(gains[:, :, :].rearrange("p a b -> p (a b)"), ps[:, 0, 0:P], ACT.Copy).then_inc(g_ready, 1)
            act.wait_ge(g_ready, 1)
            for c in range(PAIRS):
                act.wait_ge(x_ready, c + 1)
                hi_pair(0, c)
                if c < NQ:
                    w_hi(0, 0, c)
                if c:
                    square_x(0, c - 1)
            square_x(0, PAIRS - 1)
            next_hi(0, 0, (0, 1))
            act.wait_ge(state_turned, 1)
            act.activation(lnw[:, :], ps[:, 7, 0:2 * CH + 3 * CONVT], ACT.Copy).then_inc(g_ready, 1)
            act.activation(state_t.rearrange("p c b r -> p (c b r)"), ps[:, 4, 0:P], ACT.Copy).then_inc(state_ready, 1)
            act.dma_start(io["new_conv_sample"][0, :, 0, :], io["state_conv"][0, :, 1, :]).then_inc(kv_stored, 16)
            next_hi(0, 0, (2, 3))
            root(*norm_bufs(acc_pre)[:3])

            def even_task(n, q):
                if (n, q) == (N_CONV, 1):
                    act.wait_ge(kv_turned, 1)
                    keys = ps[:, 4, :].rearrange("p (a b) -> p a b", a=QT)
                    act.activation(k_tok[:, :, 0:KVW], keys, ACT.Copy).then_inc(kv_copied, 1)
                    act.activation(k_tok[:, :, KVW:], keys[:, :, 0:HD], ACT.Copy).then_inc(kv_copied, 1)
                    act.activation(v_tok.rearrange("p a b -> p (a b)"), ps[:, 5, :], ACT.Copy).then_inc(kv_copied, 1)
                    act.activation(kv_new[0:NB].rearrange("p a b -> p (a b)"), ps[0:NB, 6, :], ACT.Copy
                                   ).then_inc(kv_copied, 1)
                    act.wait_ge(kv_copied, 4)
                    act.wait_ge(win_in, 64)
                    act.dma_start(k_win[P - 1:P, :, 0:KVW], kv_new[0:NB, 0, :]).then_inc(new_in, 16)
                    act.dma_start(v_win[P - 1:P, :, :], kv_new[0:NB, 1, :]).then_inc(new_in, 16)
                    act.dma_start(io["new_k_win_prompt"][0, 0].rearrange("s g d -> s (g d)"), k_tok[:, QT - 1, 0:KVW]
                                  ).then_inc(kv_stored, 16)
                    act.dma_start(io["new_v_win_prompt"][0, 0].rearrange("s g d -> s (g d)"), v_tok[:, QT - 1, :]
                                  ).then_inc(kv_stored, 16)
                if (n, q) == (N_CONV, 3):
                    act.wait_ge(k2_turned, 1)
                    act.activation(kt2.rearrange("p a b -> p (a b)"), ps_s.rearrange("p a b -> p (a b)"), ACT.Copy
                                   ).then_inc(k2_ready, 1)
                if N_SAMP <= n < N_SAMP + 2:
                    b = NQ * (n - N_SAMP) + q
                    act.wait_ge(win_turned, b + 1)
                    if b >= 2:
                        act.wait_ge(win_scored, b - 1)
                    act.activation(kt_win[:, b % 2], ps_t.rearrange("p (a b) -> p a b", a=NKV), ACT.Copy
                                   ).then_inc(win_copied, 1)
                    if b == 0:
                        act.wait_ge(new_in, 32)
                        act.dma_start(io["new_k_win_sample"][0].rearrange("b s g d -> s b (g d)"), k_win[:, :, 0:KVW]
                                      ).then_inc(kv_stored, 16)
                        act.dma_start(io["new_v_win_sample"][0].rearrange("b s g d -> s b (g d)"), v_win[:, :, :]
                                      ).then_inc(kv_stored, 16)
                if (n, q) == (N_PR, 2):
                    act.wait_ge(s_max, 1)
                    act.activation(p_s[:, :], ps_t[:, 0:P], ACT.Exp, bias=small[:, 1:2], accum_out=small[:, 3:4]
                                   ).then_inc(s_exp, 1)
                    act.activation(small[:, 4:5], small[:, 2:3], ACT.Exp).then_inc(s_exp, 1)
                if (n, q) == (N_PR + 1, 1):
                    act.wait_ge(s_pturned, 1)
                    act.activation(pt_s[:, :], ps_t[:, 0:P], ACT.Copy).then_inc(s_pt, 1)
                if (n, q) == (N_PR + 2, 1):
                    act.wait_ge(s_pv, 1)
                    values = ps_v[:, 0:P].rearrange("p (e b c h a) -> p e h c a b", e=2, b=NB, c=2, h=2)
                    dst = attn_s.rearrange("p (c h a) b -> p h c a b", c=2, h=2)
                    for e in range(2):
                        for h in range(2):
                            ins = act.activation(dst[HD * e:HD * e + HD, h], values[HD * h:HD * h + HD, e, h], ACT.Copy)
                    ins.then_inc(s_moved, 1)
                    act.wait_ge(s_moved, 1)
                    act.activation(ahi[:, 0:8, SEQ:], attn_s[:, :, :], ACT.Copy).then_inc(s_hi, 1)
                if q == 2 and N_PR < n < N_PR + 9:
                    it = n - N_PR - 1
                    for kb in range(1 + it % 2):
                        act.wait_ge(p_turned, it // 2 * 3 + (it % 2) + kb + 1)
                        if kb == 0 and it:
                            act.wait_ge(pv_done, it)
                        act.activation(PT[:, kb], (ps_t, ps_v)[kb].rearrange("p (a b) -> p a b", a=4), ACT.Copy
                                       ).then_inc(p_copied, 1)
                if q == 2 and N_PR <= n < N_PR + 8:
                    it = n - N_PR
                    w = (1 + it % 2) * P
                    act.wait_ge(masked, it + 1)
                    for e in range(2):
                        for jj in range(2):
                            j = 2 * e + jj
                            ins = act.activation(S[:, e, jj, 0:w], S[:, e, jj, 0:w], ACT.Exp,
                                                 bias=small[:, 12 + j:13 + j], accum_out=small[:, 24 + j:25 + j])
                    act.activation(small[:, 28:32], small[:, 20:24], ACT.Exp).then_inc(p_exp, 1)
                if q == 3 and N_PR < n < N_PR + 9:
                    it = n - N_PR - 1
                    g, qi = divmod(it, 2)
                    act.wait_ge(pv_done, it + 1)
                    act.activation(ahi[:, 2 * g:2 * g + 2, qi * P:qi * P + P],
                                   ps_v[:, 0:2 * P].rearrange("p (a b) -> p a b", a=2), ACT.Copy).then_inc(attn_hi, 1)

            def conv_result(i):
                act.wait_ge(conv_done, i + 1)
                act.activation(ahi[:, 8 + 2 * i:10 + 2 * i, :], y[:, 14:16, :], ACT.Copy).then_inc(conv_hi, 1)

            for n in range(N_EOUT):
                for q in range(NQ if n else 0):
                    next_hi(n // 2, n % 2, (q,))
                    if n > N_CONV and (n - N_CONV) % 3 == 0 and q == NQ - 1:
                        conv_result((n - N_CONV) // 3 - 1)
                    even_task(n, q)
                if n < N_V:
                    act.wait_ge(w_used, 4 * n + 4)
                    if n:
                        act.wait_ge(taken, n)
                    for s in range(4):
                        ins = act.activation(swp[32 * s:32 * s + 32], pair(n % 2)[32 * (s ^ 1):32 * (s ^ 1) + 32],
                                             ACT.Copy)
                    ins.then_inc(swap_ready, 1)
                i, kind = divmod(n - N_CONV, 3)
                if n >= N_CONV and kind == 2:
                    act.wait_ge(z_ready, i + 1)
                    if i:
                        act.wait_ge(conv_ready, i)
                    for t in range(2):
                        ins = act.activation(y[:, 14 + t, 0:SEQ], z[:, t, 0:SEQ], ACT.Copy,
                                             scale=conv_w[:, 0, 2 * i + t:2 * i + t + 1])
                    ins.then_inc(tap0_ready, 1)
            conv_result(CONVT // 2 - 1)

            def ws_copy(r):
                act.wait_ge(ws_turned, r + 1)
                act.activation(ws_t[:, 8 * r:8 * r + 8, :].rearrange("p a b -> p (a b)"),
                               ps_s.rearrange("p a b -> p (a b)"), ACT.Copy).then_inc(ws_ready, 1)
                if r:
                    act.activation(ws00[:, :], ps[:, 6, 0:CH], ACT.Copy, scale=float(D)).then_inc(ws_ready, 1)

            def product_with_norm(n0, k, followed=True):
                with act.Fori(0, UNIT // 2 - 1) as i:
                    for par in range(2):
                        next_hi(n0 // 2 + i, par)
                        square_y(n0 + 2 * i + par, par, k, 2 * i + par)
                n = n0 + UNIT - 2
                for q in range(NQ):
                    next_hi(n // 2, 0, (q,))
                    if not followed:
                        act.wait_ge(xt_turned, q + 1)
                        for t in range(3):
                            act.activation(out_tok[:, t, CHUNK * q:CHUNK * q + CHUNK], ps[:, 4 + t, :], ACT.Copy
                                           ).then_inc(xt_copied, 1)
                square_y(n, 0, k, UNIT - 2)
                if followed:
                    next_hi(n // 2, 1, (0, 1, 2))
                square_y(n + 1, 1, k, UNIT - 1)
                if followed:
                    root(*norm_bufs(acc_post)[:3])
                    if k == 1:
                        ws_copy(0)
                    next_hi(n // 2, 1, (3,))
                    if k == 1:
                        ws_copy(1)
                else:
                    root(var_tok, root_tok, sq_tok)

            def up_blocks(P0, k=None):
                with act.Fori(0, UNIT // 2) as i:
                    for par in range(2):
                        next_hi(P0 + i, par, (0,))
                        if k is not None:
                            s0 = PRE[k][0]
                            act.wait_ge(sq_used, s0 + 2 * i + par - 1)
                            act.activation(sq[:, (s0 + par) % 2], x[:, bass.ds(4 * i + 2 * par, 2), :], ACT.Square
                                           ).then_inc(sq_ready, 1)
                        next_hi(P0 + i, par, (1, 2, 3))
                        act.wait_ge(taken, 2 * (P0 + i) + par + 1)
                        act.activation(asq[:, :, :], relu[:, :, :], ACT.Square).then_inc(asq_ready, 1)
                        act.activation(ahi[:, bass.ds(4 * i + 2 * par, 2), :], relu[:, :, :], ACT.Square
                                       ).then_inc(asq_ready, 1)

            def store_z():
                act.activation(z_tok[0:2 + NB, :], ps[0:2 + NB, 4:6, :].rearrange("p a b -> p (a b)"), ACT.Copy
                               ).then_inc(z_out, 1)
                act.wait_ge(z_out, 1)
                act.dma_start(io["new_conv_prompt"][0, 0], z_tok[0:2, :]).then_inc(kv_stored, 16)
                act.dma_start(io["new_conv_sample"][0, :, 1, :], z_tok[2:2 + NB, :]).then_inc(kv_stored, 16)

            def load_ws():
                act.wait_ge(kv_stored, 16 * 7)
                act.wait_ge(s_attn, 1)
                act.wait_ge(attn_ready, 8)
                act.dma_start(ws_raw[:, :, :], io["w_spatial"][0].rearrange("g t s -> t g s")).then_inc(ws_in, 16)
                act.dma_start(b_bc[:, :, :], io["b_spatial"][0].partition_broadcast(P)).then_inc(bias_in, 16)

            def ffn(l, n0, last):
                P0 = n0 // 2
                for j0, j1 in ((0, 1), (1, 2), (2, FG - 1)) if l == 0 else ((0, FG - 1),):
                    with act.Fori(j0, j1) as j:
                        up_blocks(P0 + UNIT * j)
                        with act.Fori(0, UNIT // 2) as i:
                            for par in range(2):
                                next_hi(P0 + UNIT * j + UNIT // 2 + i, par)
                    if l == 0 and j0 == 0:
                        store_z()
                    if l == 0 and j0 == 1:
                        load_ws()
                P0 = P0 + UNIT * (FG - 1)
                up_blocks(P0, 2 * l + 1)
                product_with_norm(2 * P0 + UNIT, 2 * l + 1, not last)

            product_with_norm(N_EOUT, 0)
            norm_residual(0)
            act.wait_ge(z_turned, 1)
            ffn(0, N_FFN[0], False)
            norm_residual(1)

            def gelu_v(i):
                act.activation(y[:, bass.ds(2 * i, 2), :], y[:, bass.ds(2 * i, 2), :], ACT.Gelu).then_inc(gelu_ready, 1)

            def gated_cut(c):
                act.wait_ge(gated_ready, c + 1)
                act.activation(ahi[:, 2 * c:2 * c + 2, :], u[:, 2 * c:2 * c + 2, :], ACT.Copy).then_inc(gated_hi, 1)

            for c in range(PAIRS):
                if c < NQ:
                    next_hi(N_CIN // 2, 0, (c,))
                square_x(2, c)
            next_hi(N_CIN // 2, 1)
            root(*norm_bufs(acc_pre)[:3])
            for i in range(2):
                act.wait_ge(v_scaled, i + 1)
                gelu_v(i)
            with act.Fori(1, UNIT // 2) as i:
                for par in range(2):
                    next_hi(N_CIN // 2 + i, par)
                    act.wait_ge(taken, N_CIN + 2 * i + par + 1)
                    gelu_v(2 * i + par)
            for b in range(UNIT):
                n = N_CIN + UNIT + b
                for q in range(NQ):
                    g = group_at(b, q)
                    next_hi(n // 2, n % 2, (q,))
                    if b == 0:
                        for c in (2 * q, 2 * q + 1):
                            act.wait_ge(centred, c + 1)
                            act.wait_ge(sq_used, SQ_LN + c - 1)
                            act.activation(sq[:, c % 2], y[:, 2 * c:2 * c + 2, :], ACT.Square).then_inc(sq_ready, 1)
                    if (b, q) == (1, 3):
                        root(*norm_bufs(acc_pre)[:3])
                    if 0 <= g < CH:
                        act.wait_ge(v_turned, g + 1)
                        if g >= 2:
                            act.wait_ge(mixed, g - 1)
                            act.wait_ge(v_stored[g % 2], 32 * (g // 2))
                        act.activation(vt[:, g % 2, 0:2, :], ps_t[:, 0:2 * P].rearrange("p (a b) -> p a b", a=2),
                                       ACT.Copy).then_inc(v_copied, 1)
                        act.activation(vt[0:NB, g % 2, 2, :], ps_t[0:NB, 2 * P:3 * P], ACT.Copy).then_inc(v_copied, 1)
                        act.wait_ge(v_copied, 2 * g + 2)
                        cols = slice(g * P, g * P + P)
                        act.dma_start(io["new_cmlp_v_prompt"][0, 0, :, cols], vt[:, g % 2, 1, :]
                                      ).then_inc(v_stored[g % 2], 16)
                        act.dma_start(io["new_cmlp_v_sample"][0, :, 0, cols], vt[0:NB, g % 2, 2, :]
                                      ).then_inc(v_stored[g % 2], 16)
                    if 0 <= g + 1 < CH:
                        act.wait_ge(ln_scaled, g + 2)
                        act.activation(y[:, g + 1, :], y[:, g + 1, :], ACT.Identity, bias=ln_b[:, g + 1:g + 2]
                                       ).then_inc(v_ready, 1)
                    if (b, q) in GATE_AT:
                        gated_cut(GATE_AT[b, q])
                act.wait_ge(taken, n + 1)
                act.activation(u[:, 2 * b:2 * b + 2, :], u[:, 2 * b:2 * b + 2, :], ACT.Gelu).then_inc(gelu_ready, 1)
            gated_cut(PAIRS - 1)
            product_with_norm(N_COUT, 2)
            norm_residual(2)
            for slot in range(2):
                act.wait_ge(v_stored[slot], 32 * CH // 2)
            ffn(1, N_FFN[1], True)
            act.wait_ge(factor_ready, 1)
            for c in range(3):
                act.wait_ge(y_turned, 3 * c + 3)
                act.activation(y_tok[:, CHUNK * c:CHUNK * c + CHUNK], ps[:, Y_BANK[3 * c + 2], :], ACT.Copy,
                               scale=factor_tok[:, 2:3]).then_inc(y_scaled, 1)

        @block.vector
        def _(dve):
            done = [0]
            stats = [0]

            def step(ins):
                done[0] += 1
                ins.then_inc(chain, 1)
                dve.wait_ge(chain, done[0])

            def w_lo(P2, par, q):
                dve.wait_ge(w_hi_ready, 8 * P2 + 4 * par + q + 1)
                k = slice(QK * (q % 2), QK * (q % 2) + QK)
                dve.tensor_tensor(wlo[:, QK * q:QK * q + QK, :], raw[:, 2 * par + q // 2, k, :],
                                  whi[:, QK * q:QK * q + QK, :].bitcast(F32), ALU.subtract).then_inc(w_lo_ready, 1)

            def next_lo(P2, par, qs):
                for q in qs:
                    w_lo(P2 + par, 1 - par, q)

            def rsqrt(out, st, mean, v, s, w, scratch, pre=None):
                dve.wait_ge(stat_ready, st + 1)
                if pre is None:
                    ins = dve.tensor_scalar(v, mean, EPS, None, ALU.add)
                else:
                    ins = dve.scalar_tensor_tensor(out=v, in0=pre, scalar=EPS, in1=mean, op0=ALU.mult, op1=ALU.add)
                ins.then_inc(var_ready, 1)
                stats[0] += 1
                dve.wait_ge(var_ready, stats[0])
                step(dve.reciprocal(out, v))
                dve.wait_ge(root_ready, 2 * stats[0])
                dve.scalar_tensor_tensor(out=scratch, in0=w, scalar=-0.5, in1=out, op0=ALU.mult, op1=ALU.mult)
                step(dve.tensor_tensor(s, s, out, ALU.mult))
                return dve.scalar_tensor_tensor(out=out, in0=scratch, scalar=1.5, in1=s, op0=ALU.add, op1=ALU.mult)

            def lo_tile(k, t):
                ins = dve.scalar_tensor_tensor(out=hlo[:, t, :], in0=x[:, t, :], scalar=gains[:, G_PRE[k], t:t + 1],
                                               in1=hhi[:, t, :].bitcast(F32), op0=ALU.mult, op1=ALU.subtract)
                if t == 0:
                    ins.then_inc(h_first, 1)
                elif t % 2:
                    ins.then_inc(h_ready, 1)

            def lo_pair(k, c):
                dve.wait_ge(h_hi_ready, PAIRS * k + c + 1)
                lo_tile(k, 2 * c)
                lo_tile(k, 2 * c + 1)

            def norm_residual(k, homogeneous, next_n):
                rsqrt(rs_post[:, :], MIX_POST[k][1], ps_stat, *norm_bufs(acc_post),
                      pre=rs_pre[:, :] if homogeneous else None).then_inc(post_ready, 1)
                dve.wait_ge(post_ready, k + 1)

                def scale(c):
                    dve.wait_ge(gained, PAIRS * k + c + 1)
                    dve.tensor_tensor(y[:, 2 * c:2 * c + 2, :], y[:, 2 * c:2 * c + 2, :], twice(rs_post[:, :]), ALU.mult
                                      ).then_inc(scaled, 1)

                dve.wait_ge(gained, PAIRS * k + 1)
                for t in range(2):
                    step(dve.tensor_tensor(y[:, t, :], y[:, t, :], rs_post[:, :], ALU.mult))
                    dve.tensor_tensor(x[:, t, :], x[:, t, :], y[:, t, :], ALU.add).then_inc(x_added_v, 1)
                dve.wait_ge(h_hi_first, k + 2)
                lo_tile(k + 1, 0)
                scale(2)
                dve.wait_ge(h_hi_ready, PAIRS * (k + 1) + 1)
                lo_tile(k + 1, 1)
                scale(3)
                for c in range(1, PAIRS):
                    lo_pair(k + 1, c)
                    if c + 3 < PAIRS:
                        scale(c + 3)
                    if c == 5:
                        w_lo(next_n // 2, 0, NQ - 1)

            for c in range(PAIRS + 1):
                if c < PAIRS:
                    dve.wait_ge(x_turned, c + 1)
                    dve.tensor_copy(x[:, 2 * c:2 * c + 2, :], ps[:, 2 + 2 * (c % 3):4 + 2 * (c % 3), 0:T]
                                    ).then_inc(x_ready, 1)
                if c >= 2:
                    lo_pair(0, c - 2)
                if 2 <= c < 2 + NQ:
                    w_lo(0, 0, c - 2)
            lo_pair(0, PAIRS - 1)
            next_lo(0, 0, (0, 1))
            dve.wait_ge(sinks_in, 16)
            dve.wait_ge(state_ready, 1)
            for e in range(2):
                ins = dve.tensor_copy(sink_r[:, 64 * e:64 * e + 64].rearrange("p (b a) -> p b a", b=NB),
                                      sinks[:, :].rearrange("p (a e) -> p e a", e=2)[:, e, :].unsqueeze(1)
                                      .to_broadcast([P, NB, 8]))
            ins.then_inc(sink_ready, 1)
            next_lo(0, 0, (2, 3))
            step(rsqrt(rs_pre[:, :], ST_X0, ps_stat, *norm_bufs(acc_pre)))
            dve.wait_ge(rope_in, 32)
            step(dve.tensor_tensor(cos[:, :], cos[:, :], rs_pre[:, :], ALU.mult))
            step(dve.tensor_tensor(sin[:, :], sin[:, :], rs_pre[:, :], ALU.mult))

            def even_task(n, q):
                if (n, q) == (N_PR, 0):
                    dve.wait_ge(win_scored, NB)
                    src = ps[:, 4, 0:P].rearrange("p (e b a) -> p e b a", e=2, b=NB)
                    dst = sc_s.rearrange("p (e b a) -> p e b a", e=2, b=NB)
                    dve.tensor_scalar(dst[:, 0], src[:, 0], SCALE, None, ALU.mult)
                    dve.tensor_scalar(dst[:, 1, :, 2:8], src[:, 1, :, 0:6], SCALE, None, ALU.mult)
                    dve.tensor_scalar(dst[:, 1, :, 0:2], src[:, 1, :, 6:8], SCALE, None, ALU.mult).then_inc(sc_ready, 1)
                if (n, q) == (N_CONV, 2):
                    dve.wait_ge(q_zeroed, 1)
                    dve.tensor_copy(q_samp[0:HD, 0], y[0:HD, 0:8, SEQ:])
                    dve.tensor_copy(q_samp[HD:, 1, 0:6], y[HD:, 2:8, SEQ:])
                    dve.tensor_copy(q_samp[HD:, 1, 6:8], y[HD:, 0:2, SEQ:]).then_inc(q_samp_ready, 1)
                if (n, q) == (2, 0):
                    dve.wait_ge(sink_turned, 1)
                    step(dve.tensor_copy(small[:, 0:1], ps[:, 5, 0:1]))
                if (n, q) == (N_PR, 1):
                    dve.wait_ge(sc_turned, 1)
                    step(dve.tensor_reduce(small[:, 1:2], ps_t[:, 0:P], AX.X, ALU.max))
                    step(dve.tensor_tensor(small[:, 1:2], small[:, 1:2], small[:, 0:1], ALU.max))
                    step(dve.tensor_scalar(small[:, 1:2], small[:, 1:2], -1.0, None, ALU.mult))
                    dve.tensor_tensor(small[:, 2:3], small[:, 0:1], small[:, 1:2], ALU.add).then_inc(s_max, 1)
                if (n, q) == (N_PR, 3):
                    dve.wait_ge(s_exp, 2)
                    step(dve.tensor_tensor(small[:, 5:6], small[:, 3:4], small[:, 4:5], ALU.add))
                    step(dve.reciprocal(small[:, 6:7], small[:, 5:6]))
                    dve.tensor_scalar(p_s[:, :], p_s[:, :], small[:, 6:7], None, ALU.mult).then_inc(s_prob, 1)
                if (n, q) == (N_PR + 2, 1):
                    dve.wait_ge(s_hi, 1)
                    dve.tensor_tensor(alo[:, 0:8, SEQ:], attn_s[:, :, :],
                                      ahi[:, 0:8, SEQ:].bitcast(F32), ALU.subtract).then_inc(s_attn, 1)
                if q == 2 and N_PR <= n < N_PR + 8:
                    it = n - N_PR
                    g, qi = divmod(it, 2)
                    w = (1 + qi) * P
                    dve.wait_ge(scored, it + 1)
                    if it == 0:
                        dve.wait_ge(mask_ready, 1)
                    for e in range(2):
                        ins = dve.scalar_tensor_tensor(
                            out=S[:, e, :, 0:w], in0=ps_s[:, e, :].rearrange("p (a b) -> p a b", a=2)[:, :, 0:w],
                            scalar=SCALE, in1=mask[:, 2 * P - w:].unsqueeze(1).to_broadcast([P, 2, w]), op0=ALU.mult,
                            op1=ALU.add)
                    step(ins)
                    step(dve.tensor_reduce(small[:, 8:12], S.rearrange("p e a b -> p (e a) b")[:, :, 0:w], AX.X,
                                           ALU.max))
                    sink = sinks[:, GQA * g:GQA * g + GQA].rearrange("p (a e) -> p e a", e=2)
                    m4 = small[:, 8:12].rearrange("p (e a) -> p e a", e=2)
                    step(dve.tensor_tensor(m4, m4, sink, ALU.max))
                    step(dve.tensor_scalar(small[:, 12:16], small[:, 8:12], -1.0, None, ALU.mult))
                    dve.tensor_tensor(small[:, 20:24].rearrange("p (e a) -> p e a", e=2), sink,
                                      small[:, 12:16].rearrange("p (e a) -> p e a", e=2), ALU.add
                                      ).then_inc(masked, 1)
                if q == 3 and N_PR <= n < N_PR + 8:
                    it = n - N_PR
                    dve.wait_ge(p_exp, it + 1)
                    step(dve.tensor_tensor(small[:, 32:36], small[:, 24:28], small[:, 28:32], ALU.add))
                    dve.reciprocal(small[:, 16:20], small[:, 32:36]).then_inc(p_rec, 1)
                if q == 3 and N_PR < n < N_PR + 9:
                    it = n - N_PR - 1
                    g, qi = divmod(it, 2)
                    dve.wait_ge(attn_hi, it + 1)
                    dve.tensor_tensor(alo[:, 2 * g:2 * g + 2, qi * P:qi * P + P],
                                      ps_v[:, 0:2 * P].rearrange("p (a b) -> p a b", a=2),
                                      ahi[:, 2 * g:2 * g + 2, qi * P:qi * P + P].bitcast(F32), ALU.subtract
                                      ).then_inc(attn_ready, 1)

            def conv_taps(i):
                dve.wait_ge(tap0_ready, i + 1)
                if i == 0:
                    dve.wait_ge(conv_s_ready, 1)
                for tap in (1, 2):
                    for t in range(2):
                        ins = dve.scalar_tensor_tensor(
                            out=y[:, 14 + t, 0:SEQ], in0=z[:, t, tap:tap + SEQ],
                            scalar=conv_w[:, tap, 2 * i + t:2 * i + t + 1], in1=y[:, 14 + t, 0:SEQ], op0=ALU.mult,
                            op1=ALU.add)
                    step(ins)
                for t in range(2):
                    ins = dve.scalar_tensor_tensor(
                        out=y[:, 14 + t, SEQ:], in0=z[:, t, 2 + SEQ:], scalar=conv_w[:, 2, 2 * i + t:2 * i + t + 1],
                        in1=conv_s[:, 2 * i + t, :], op0=ALU.mult, op1=ALU.add)
                step(ins)

            def conv_gate(i):
                dve.tensor_tensor(y[:, 14:16, :], y[:, 14:16, :], y[:, 12:14, :], ALU.mult).then_inc(conv_done, 1)

            def conv_lo(i):
                dve.wait_ge(conv_hi, i + 1)
                dve.tensor_tensor(alo[:, 8 + 2 * i:10 + 2 * i, :], y[:, 14:16, :],
                                  ahi[:, 8 + 2 * i:10 + 2 * i, :].bitcast(F32), ALU.subtract).then_inc(conv_ready, 1)

            CONV_STEPS = {0: conv_taps, 1: conv_gate, 3: conv_lo}

            def conv_task(n, q):
                if n > N_CONV and (n - N_CONV) % 3 == 0 and q in CONV_STEPS:
                    CONV_STEPS[q]((n - N_CONV) // 3 - 1)

            for n in range(N_EOUT):
                par = n % 2
                for q in range(NQ - 1 if n else 0):
                    next_lo(n // 2, par, (q,))
                    even_task(n, q)
                    conv_task(n, q)
                i, kind = divmod(n - N_CONV, 3)
                dve.wait_ge(w_used, 4 * n + 4)
                if n < N_V:
                    dst = y[:, 2 * n:2 * n + 2, :]
                    dve.wait_ge(swap_ready, n + 1)
                    dve.tensor_tensor(dst, pair(par), twice(cos[:, :]), ALU.mult)
                    step(dve.tensor_tensor(swp[:, :, :], swp[:, :, :], twice(sin[:, :]), ALU.mult))
                    dve.tensor_tensor(dst, dst, swp[:, :, :], ALU.add).then_inc(taken, 1)
                elif n == N_V:
                    dve.tensor_tensor(y[:, 10:12, :], pair(par), twice(rs_pre[:, :]), ALU.mult).then_inc(taken, 1)
                else:
                    if n == N_CONV:
                        dve.wait_ge(kv_turned, 1)
                    if i and kind < 2:
                        dve.wait_ge(z_ready, i)
                    t = 8 + 2 * kind
                    dve.tensor_tensor(y[:, t:t + 2, :], pair(par), twice(rs_pre[:, :]), ALU.mult).then_inc(taken, 1)
                if n:
                    next_lo(n // 2, par, (NQ - 1,))
                    even_task(n, NQ - 1)
                    conv_task(n, NQ - 1)
            for conv_step in CONV_STEPS.values():
                conv_step(CONVT // 2 - 1)

            def take_block(P2, par, i, add, quarters_after=(NQ - 1,), tail=False):
                if quarters_after is not None:
                    next_lo(P2, par, (0, 1, 2))
                dve.wait_ge(w_used, 8 * P2 + 4 * par + 4)
                def take(dst, src):
                    return dve.tensor_tensor(dst, dst, src, ALU.add) if add else dve.tensor_copy(dst, src)

                if tail:
                    take(y[:, 2 * i, :], pair(par)[:, 0, :]).then_inc(tail_taken, 1)
                    take(y[:, 2 * i + 1, :], pair(par)[:, 1, :]).then_inc(taken, 1)
                else:
                    take(y[:, bass.ds(2 * i, 2), :], pair(par)).then_inc(taken, 1)
                if quarters_after:
                    next_lo(P2, par, quarters_after)

            def product_before_norm(n0, add, last=False):
                P0 = n0 // 2
                with dve.Fori(0, UNIT // 2 - 1) as i:
                    for par in range(2):
                        take_block(P0 + i, par, 2 * i + par, add)
                take_block(P0 + UNIT // 2 - 1, 0, UNIT - 2, add)
                take_block(P0 + UNIT // 2 - 1, 1, UNIT - 1, add, None if last else (), tail=True)

            def up_blocks(P0, m0):
                with dve.Fori(0, UNIT // 2) as i:
                    for par in range(2):
                        m = m0 + 2 * i + par
                        next_lo(P0 + i, par, (0, 1, 2))
                        dve.wait_ge(w_used, 8 * (P0 + i) + 4 * par + 4)
                        dve.tensor_scalar(relu[:, :, :], pair(par), 0.0, None, ALU.max).then_inc(taken, 1)
                        next_lo(P0 + i, par, (3,))
                        dve.wait_ge(asq_ready, 2 * m + 2)
                        dve.tensor_tensor(alo[:, bass.ds(4 * i + 2 * par, 2), :], asq[:, :, :],
                                          ahi[:, bass.ds(4 * i + 2 * par, 2), :].bitcast(F32), ALU.subtract
                                          ).then_inc(a_ready, 1)

            def ffn(l, n0, last):
                P0, m0 = n0 // 2, FG * UNIT * l
                with dve.Fori(0, FG - 1) as j:
                    up_blocks(P0 + UNIT * j, m0 + UNIT * j)
                    dve.wait_ge(y_zero, l + 1)
                    with dve.Fori(0, UNIT // 2) as i:
                        for par in range(2):
                            take_block(P0 + UNIT * j + UNIT // 2 + i, par, 2 * i + par, True)
                P0, m0 = P0 + UNIT * (FG - 1), m0 + UNIT * (FG - 1)
                up_blocks(P0, m0)
                dve.wait_ge(stat_ready, PRE[2 * l + 1][1] + 1)
                if last:
                    step(dve.tensor_scalar(var_tok, ps[:, 7, 0:3], EPS, None, ALU.add))
                    step(dve.tensor_tensor(pre_tok, var_tok, var_tok, ALU.mult))
                else:
                    step(dve.tensor_scalar(tmp[:, :], ps_stat, EPS, None, ALU.add))
                    step(dve.tensor_tensor(rs_pre[:, :], tmp[:, :], tmp[:, :], ALU.mult))
                product_before_norm(2 * P0 + UNIT, True, last)

            product_before_norm(N_EOUT, False)
            norm_residual(0, False, N_FFN[0])
            ffn(0, N_FFN[0], False)
            norm_residual(1, True, N_CIN)

            def scale_v(n, par, i):
                dve.wait_ge(w_used, 4 * n + 4)
                dve.tensor_tensor(y[:, bass.ds(2 * i, 2), :], pair(par), twice(rs_pre[:, :]), ALU.mult
                                  ).then_inc(taken, 1)

            wait_added(dve, 1, 0)
            wait_added(dve, 1, 1)
            for par in range(2):
                take_block(N_CIN // 2, par, par, False)
            step(rsqrt(rs_pre[:, :], ST_PRE2, ps_stat, *norm_bufs(acc_pre)))
            for c in range(2):
                pair_y = y[:, 2 * c:2 * c + 2, :]
                dve.tensor_tensor(pair_y, pair_y, twice(rs_pre[:, :]), ALU.mult).then_inc(v_scaled, 1)
            wait_added(dve, 1, PAIRS - 1)
            with dve.Fori(1, UNIT // 2) as i:
                for par in range(2):
                    next_lo(N_CIN // 2 + i, par, (0, 1, 2))
                    scale_v(N_CIN + 2 * i + par, par, 2 * i + par)
                    next_lo(N_CIN // 2 + i, par, (3,))
            def gate(c):
                dve.wait_ge(gelu_ready, UNIT + c + 1)
                dve.wait_ge(mix_ready, 2 * c + 2)
                dve.tensor_tensor(u[:, 2 * c:2 * c + 2, :], u[:, 2 * c:2 * c + 2, :], y[:, 2 * c:2 * c + 2, :],
                                  ALU.mult).then_inc(gated_ready, 1)

            def gated_lo(c):
                dve.wait_ge(gated_hi, c + 1)
                dve.tensor_tensor(alo[:, 2 * c:2 * c + 2, :], u[:, 2 * c:2 * c + 2, :],
                                  ahi[:, 2 * c:2 * c + 2, :].bitcast(F32), ALU.subtract).then_inc(g_lo_ready, 1)

            for b in range(UNIT):
                n = N_CIN + UNIT + b
                par = n % 2
                for q in range(NQ):
                    g = group_at(b, q)
                    if q == NQ - 1:
                        dve.wait_ge(w_used, 4 * n + 4)
                        dve.tensor_tensor(u[:, 2 * b:2 * b + 2, :], pair(par), twice(rs_pre[:, :]), ALU.mult
                                          ).then_inc(taken, 1)
                    if 0 < g <= CH:
                        dve.wait_ge(mixed, g)
                        if g == 1:
                            dve.wait_ge(bias_in, 16)
                            dve.wait_ge(ws_ready, 3)
                        dve.tensor_scalar(y[:, g - 1, SEQ:], y[:, g - 1, SEQ:], ws00[:, g - 1:g],
                                          b_bc[:, g - 1, 0:1], ALU.mult, ALU.add)
                        dve.tensor_tensor(y[:, g - 1, 0:SEQ].rearrange("p (a b) -> p a b", a=2),
                                          ps_v[:, 0:SEQ].rearrange("p (a b) -> p a b", a=2),
                                          twice(b_bc[:, g - 1, :]), ALU.add).then_inc(mix_ready, 1)
                    if 0 <= g + 1 < CH:
                        dve.scalar_tensor_tensor(out=y[:, g + 1, :], in0=y[:, g + 1, :], scalar=ln_g[:, g + 1:g + 2],
                                                 in1=rs_post[:, :], op0=ALU.mult, op1=ALU.mult).then_inc(ln_scaled, 1)
                    next_lo(n // 2, par, (q,))
                    if b == 0:
                        if q == 0:
                            dve.wait_ge(stat_ready, ST_MEAN + 1)
                            step(dve.tensor_copy(rs_post[:, :], ps_stat))
                        for c in (2 * q, 2 * q + 1):
                            dve.wait_ge(gelu_ready, c + 1)
                            dve.tensor_tensor(y[:, 2 * c:2 * c + 2, :], y[:, 2 * c:2 * c + 2, :],
                                              twice(rs_post[:, :]), ALU.subtract).then_inc(centred, 1)
                    if (b, q) == (1, 3):
                        step(rsqrt(rs_post[:, :], ST_LN, ps_stat, *norm_bufs(acc_pre)))
                    if (b, q) in GATE_AT:
                        gate(GATE_AT[b, q])
                    if (b, q) in CUT_AT:
                        gated_lo(CUT_AT[b, q])
            gate(PAIRS - 1)
            gated_lo(PAIRS - 1)
            product_before_norm(N_COUT, False)
            norm_residual(2, False, N_FFN[1])
            ffn(1, N_FFN[1], True)
            dve.wait_ge(stat_ready, MIX_POST[3][1] + 1)
            step(dve.tensor_copy(sum_tok, ps[:, 7, 0:3]))
            step(dve.tensor_tensor(sum_tok, sum_tok, ps[:, 7, 3:6], ALU.add))
            rsqrt(factor_tok, MIX_POST[3][1], sum_tok, var_tok, root_tok, sq_tok, corr_tok, pre_tok
                  ).then_inc(factor_ready, 1)
            dve.wait_ge(factor_ready, 1)
            dve.wait_ge(xt_copied, 12)
            for c in range(4):
                for t in range(QT if c < 3 else 3):
                    dst = out_tok[:, t, CHUNK * c:CHUNK * c + CHUNK]
                    dve.wait_ge(y_turned, 3 * c + t + 1)
                    dve.scalar_tensor_tensor(out=dst, in0=ps[:, Y_BANK[3 * c + t], :], scalar=factor_tok[:, t:t + 1],
                                             in1=dst, op0=ALU.mult, op1=ALU.add).then_inc(out_ready_v, 1)

        @block.tensor
        def _(pe):
            def quarter(n, par, q, hi, lo, operand=None):
                if q == 0 and not (isinstance(n, int) and n < 2):
                    pe.wait_ge(taken, n - 1)
                pe.wait_ge(w_lo_ready, 4 * n + q + 1)
                for k in range(QK * q, QK * q + QK):
                    if operand:
                        operand(k)
                    for j in range(2):
                        cols = slice(P * j, P * j + P)
                        out = ps[:, 2 * par + j, 0:T]
                        pe.matmul(out, whi[:, k, cols], hi[:, k, :], start=(k == 0), stop=False)
                        pe.matmul(out, whi[:, k, cols], lo[:, k, :], start=False, stop=False)
                        mm = pe.matmul(out, wlo[:, k, cols], hi[:, k, :], start=False, stop=(k == CH - 1))
                mm.then_inc(w_used, 1)

            def h_operand(k_norm):
                def wait(k):
                    if k == 0:
                        pe.wait_ge(h_first, k_norm + 1)
                    elif k == 1 or k % 2 == 0:
                        pe.wait_ge(h_ready, PAIRS * k_norm + k // 2 + 1)
                return wait

            def statistic(acc, k=None):
                for j in range(2):
                    mm = pe.matmul(ps_stat, mean_w[:, :], acc[:, j, :], start=(j == 0), stop=(j == 1 and k is None))
                if k is not None:
                    for j in range(2):
                        pe.wait_ge(tail_ready, 2 * k + j + 1)
                        mm = pe.matmul(ps_stat, mean_w[:, :], sq_tail[:, j, :], start=False, stop=(j == 1))
                mm.then_inc(stat_ready, 1)

            def token_statistic(parts, column):
                for t in range(3):
                    for j in range(2):
                        mm = pe.matmul(ps[:, 7, column + t:column + t + 1], parts[:, j, TOK[t]:TOK[t] + P],
                                       mean_w[:, 0:1], start=(j == 0), stop=(j == 1))
                return mm

            def turn_x(c):
                if c >= 3:
                    pe.wait_ge(x_ready, c - 2)
                for tok in range(3):
                    if c == 0:
                        pe.wait_ge(x_in[(0, 1, 4)[tok]], 16)
                    if c == PAIRS // 2 and tok < 2:
                        pe.wait_ge(x_in[2 + tok], 16)
                    for t in range(2):
                        tile, bank = 2 * c + t, 2 + 2 * (c % 3) + t
                        cols = slice(P * tile, P * tile + P)
                        if tok < 2:
                            mm = pe.transpose(ps[:, bank, P * tok:P * tok + P], x_tok[:, tok, cols], ident[:, :])
                        else:
                            mm = pe.transpose(ps[:, bank, SEQ:T], x_tok[0:NB, 2, cols], ident[0:NB, 0:NB])
                mm.then_inc(x_turned, 1)

            pe.wait_ge(const_ready, 2)
            for c in range(3):
                turn_x(c)
            pe.wait_ge(g_in, 16 * 4)
            pe.transpose(ps[:, 0, 0:P], g_rows[:, 0, :], ident[:, :]).then_inc(g_turned, 1)
            turn_x(3)
            turn_x(4)
            for q in range(NQ):
                if q == NQ - 1:
                    pe.wait_ge(state_in, 16)
                    pe.wait_ge(l_in, 16 * 3)
                    pe.wait_ge(x_ready, PAIRS)
                    n_small = 2 * CH + 3 * CONVT
                    pe.transpose(ps[:, 7, 0:n_small], g_rows[0:n_small, 1, :], ident[0:n_small, 0:n_small])
                    for c in range(CONVT):
                        mm = pe.transpose(ps[:, 4, 16 * c:16 * c + 16], state_tok[0:2 * NB, P * c:P * c + P],
                                          ident[0:2 * NB, 0:2 * NB])
                    mm.then_inc(state_turned, 1)
                quarter(0, 0, q, hhi, hlo, h_operand(0))
                for c in {0: (5, 6), 1: (7,)}.get(q, ()):
                    turn_x(c)

            def even_task(n, q):
                if (n, q) == (1, 0):
                    pe.wait_ge(sq_used, SQ_X0 + PAIRS)
                    pe.wait_ge(g_ready, 2)
                    statistic(acc_pre)
                if (n, q) == (1, 1):
                    pe.wait_ge(sink_ready, 1)
                    pe.transpose(ps[:, 5, 0:P], sink_r[:, :], ident[:, :]).then_inc(sink_turned, 1)
                if (n, q) == (N_CONV, 1):
                    pe.wait_ge(taken, N_CONV)
                    for kv in range(2):
                        for t in range(QT):
                            for h in range(2):
                                pe.transpose(ps[:, 4 + kv, KVW * t + P * h:KVW * t + P * h + P],
                                             y[:, 8 + 2 * kv + h, P * t:P * t + P], ident[:, :])
                        for h in range(2):
                            mm = pe.transpose(ps[0:NB, 6, KVW * kv + P * h:KVW * kv + P * h + P],
                                              y[:, 8 + 2 * kv + h, SEQ:], ident[:, :])
                    mm.then_inc(kv_turned, 1)
                if (n, q) == (N_CONV, 3):
                    pe.wait_ge(kv_copied, 3)
                    for g in range(NKV):
                        for t in range(QT):
                            col = SEQ * (g % 2) + P * t
                            mm = pe.transpose(ps[:, 4 + g // 2, col:col + P],
                                              k_tok[:, t, HD * g:HD * g + P],
                                              ident[:, :])
                    mm.then_inc(k2_turned, 1)

                def win_scores(b):
                    pe.wait_ge(win_copied, b + 1)
                    if b == 0:
                        pe.wait_ge(k2_ready, 1)
                        pe.wait_ge(q_samp_ready, 1)
                    scores = ps[:, 4, 0:P].rearrange("p (e b a) -> p e b a", e=2, b=NB)
                    for g in range(NKV):
                        mm = pe.matmul(scores[:, :, b, 2 * g:2 * g + 2], kt_win[:, b % 2, g, :],
                                       q_samp[:, :, 2 * g:2 * g + 2, b], start=True, stop=True)
                    mm.then_inc(win_scored, 1)

                if N_SAMP <= n < N_SAMP + 2:
                    b = NQ * (n - N_SAMP) + q
                    if b == 0:
                        pe.wait_ge(win_ready, 1)
                        pe.wait_ge(kv_copied, 4)
                    else:
                        pe.wait_ge(win_copied, b)
                    for g in range(NKV):
                        mm = pe.transpose(ps_t[:, P * g:P * g + P],
                                          k_win[:, b, HD * g:HD * g + P],
                                          ident[:, :])
                    mm.then_inc(win_turned, 1)
                    if b:
                        win_scores(b - 1)
                if (n, q) == (N_PR, 0):
                    win_scores(NB - 1)
                if (n, q) == (N_PR, 1):
                    pe.wait_ge(sc_ready, 1)
                    pe.transpose(ps_t[:, 0:P], sc_s[:, :], ident[:, :]).then_inc(sc_turned, 1)
                if (n, q) == (N_PR + 1, 1):
                    pe.wait_ge(s_prob, 1)
                    pe.transpose(ps_t[:, 0:P], p_s[:, :], ident[:, :]).then_inc(s_pturned, 1)
                if (n, q) == (N_PR + 2, 1):
                    pe.wait_ge(s_pt, 1)
                    pe.wait_ge(attn_ready, 1)
                    cols = "p (e b a) -> p e b a"
                    for b in range(NB):
                        for gp in range(2):
                            mm = pe.matmul(ps_v[:, 0:P].rearrange(cols, e=2, b=NB)[:, :, b, 4 * gp:4 * gp + 4],
                                           v_win[:, b, P * gp:P * gp + P],
                                           pt_s.rearrange(cols, e=2, b=NB)[:, :, b, 4 * gp:4 * gp + 4],
                                           start=True, stop=True)
                    mm.then_inc(s_pv, 1)
                if q == 2 and N_PR < n < N_PR + 9:
                    it = n - N_PR - 1
                    pe.wait_ge(p_norm, it + 1)
                    if it == 0:
                        pe.wait_ge(s_pt, 1)
                    else:
                        pe.wait_ge(p_copied, it // 2 * 3 + it % 2)
                    for kb in range(1 + it % 2):
                        if kb:
                            pe.wait_ge(attn_ready, it)
                            if it == 1:
                                pe.wait_ge(s_attn, 1)
                        for e in range(2):
                            for jj in range(2):
                                col = P * (2 * e + jj)
                                mm = pe.transpose((ps_t, ps_v)[kb][:, col:col + P], S[:, e, jj, P * kb:P * kb + P],
                                                  ident[:, :])
                        mm.then_inc(p_turned, 1)
                if q == 3 and N_PR < n < N_PR + 9:
                    it = n - N_PR - 1
                    g, qi = divmod(it, 2)
                    pe.wait_ge(p_copied, it // 2 * 3 + (it % 2) * 2 + 1)
                    if it:
                        pe.wait_ge(attn_ready, it)
                    for kb in range(1 + qi):
                        for e in range(2):
                            mm = pe.matmul(ps_v[HD * e:HD * e + HD, 0:2 * P], v_tok[:, kb, HD * g:HD * g + HD],
                                           PT[:, kb, 2 * e:2 * e + 2, :], start=(kb == 0), stop=(kb == qi))
                    mm.then_inc(pv_done, 1)
                if q == 2 and N_PR <= n < N_PR + 8:
                    it = n - N_PR
                    g, qi = divmod(it, 2)
                    w = (1 + qi) * P
                    if it == 0:
                        pe.wait_ge(sc_ready, 1)
                    else:
                        pe.wait_ge(masked, it)
                    for jj in range(2):
                        for e in range(2):
                            rows_ = slice(HD * e, HD * e + HD)
                            mm = pe.matmul(ps_s[:, e, SEQ * jj:SEQ * jj + w], y[rows_, 2 * g + jj, P * qi:P * qi + P],
                                           kt2[rows_, (g - e) % NKV, 0:w], start=True, stop=True)
                    mm.then_inc(scored, 1)

            for n in range(1, N_EOUT):
                for q in range(NQ):
                    quarter(n, n % 2, q, hhi, hlo)
                    even_task(n, q)

            def attn_operand(k):
                if k == 0:
                    pe.wait_ge(s_attn, 1)
                if k in (0, 2, 4, 6):
                    pe.wait_ge(attn_ready, k + 2)
                if k >= 8 and k % 2 == 0:
                    pe.wait_ge(conv_ready, (k - 8) // 2 + 1)

            def gated_operand(k):
                if k % 2 == 0:
                    pe.wait_ge(g_lo_ready, k // 2 + 1)

            def product(n0, hi, lo, operand, pairs=UNIT // 2):
                with pe.Fori(0, pairs) as i:
                    for par in range(2):
                        for q in range(NQ):
                            quarter(n0 + 2 * i + par, par, q, hi, lo, operand if par == 0 else None)

            def post_statistic(k):
                pe.wait_ge(sq_used, MIX_POST[k][0] + TAIL)
                statistic(acc_post, k)

            product(N_EOUT, ahi, alo, attn_operand)
            pe.wait_ge(attn_ready, 8)
            post_statistic(0)
            pe.wait_ge(z_ready, 4)
            pe.wait_ge(masked, 8)
            for c in range(CONVT):
                mm = pe.transpose(ps[0:2 + NB, 4 + c // 4, P * (c % 4):P * (c % 4) + P], z_last[:, c, :], ident[:, :])
            mm.then_inc(z_turned, 1)

            def turn_ws(r):
                if r == 0:
                    pe.wait_ge(ws_masked, 1)
                    pe.wait_ge(z_out, 1)
                else:
                    pe.wait_ge(ws_ready, r)
                for g in range(8):
                    mm = pe.transpose(ps_s[:, g // 4, P * (g % 4):P * (g % 4) + P], ws_raw[:, 8 * r + g, :],
                                      ident[:, :])
                if r:
                    mm = pe.matmul(ps[:, 6, 0:CH], mean_w[0:1, :], ws_raw[0:1, :, 0], start=True, stop=True)
                mm.then_inc(ws_turned, 1)

            def ffn(l, n0):
                def up(base, m0):
                    def hidden(k):
                        if k % 2 == 0:
                            pe.wait_ge(a_ready, m0 + k // 2 + 1)
                    product(base, hhi, hlo, h_operand(2 * l + 1))
                    return hidden

                with pe.Fori(0, FG - 1) as j:
                    base = n0 + 2 * UNIT * j
                    hidden = up(base, FG * UNIT * l + UNIT * j)
                    product(base + UNIT, ahi, alo, hidden)
                base = n0 + 2 * UNIT * (FG - 1)
                hidden = up(base, FG * UNIT * l + UNIT * (FG - 1))
                pe.wait_ge(sq_used, PRE[2 * l + 1][0] + PAIRS)
                if l == 0:
                    statistic(acc_pre)
                    product(base + UNIT, ahi, alo, hidden)
                    post_statistic(1)
                    turn_ws(0)
                    turn_ws(1)
                else:
                    token_statistic(acc_pre, 0).then_inc(stat_ready, 1)
                    product(base + UNIT, ahi, alo, hidden, UNIT // 2 - 1)
                    last_blocks()

            def turn_tokens(src, c, t, bank):
                for k in range(4):
                    mm = pe.transpose(ps[:, bank, P * k:P * k + P], src[:, 4 * c + k, TOK[t]:TOK[t] + P], ident[:, :])
                return mm

            def last_blocks():
                for par in range(2):
                    for q in range(NQ):
                        quarter(N_END - 2 + par, par, q, ahi, alo)
                        if par == 0:
                            if q:
                                pe.wait_ge(xt_copied, 3 * q)
                            for t in range(3):
                                mm = turn_tokens(x, q, t, 4 + t)
                            mm.then_inc(xt_turned, 1)
                        elif q == 2:
                            pe.wait_ge(xt_copied, 12)
                            turn_y(0, range(3))
                turn_y(1, range(2))
                pe.wait_ge(sq_used, MIX_POST[3][0] + TAIL)
                token_statistic(acc_post, 0)
                pe.wait_ge(tail_ready, 8)
                token_statistic(sq_tail, 3).then_inc(stat_ready, 1)
                turn_y(1, (2,))
                for c in (2, 3):
                    turn_y(c, range(3))

            def turn_y(c, tiles):
                pe.wait_ge(gained, 3 * PAIRS + 2 * c + 2)
                for t in tiles:
                    i = 3 * c + t
                    if i in (3, 4):
                        pe.wait_ge(taken, N_END - 1)
                    if i in (5, 6):
                        pe.wait_ge(taken, N_END)
                    if i in (7, 8, 10, 11):
                        pe.wait_ge(out_ready_v, {7: 1, 8: 2, 10: 3, 11: 4}[i])
                    if i == 9:
                        pe.wait_ge(y_scaled, 1)
                    turn_tokens(y, c, t, Y_BANK[i]).then_inc(y_turned, 1)

            ffn(0, N_FFN[0])
            for par in range(2):
                for q in range(NQ):
                    quarter(N_CIN + par, par, q, hhi, hlo, h_operand(2))
            pe.wait_ge(sq_used, PRE[2][0] + PAIRS)
            statistic(acc_pre)
            product(N_CIN + 2, hhi, hlo, None, UNIT // 2 - 1)

            def v_tokens(g):
                pe.wait_ge(v_ready, g + 1)
                if g:
                    pe.wait_ge(v_copied, 2 * g)
                pe.transpose(ps_t[:, 0:P], y[:, g, 0:P], ident[:, :])
                pe.transpose(ps_t[:, P:2 * P], y[:, g, P:2 * P], ident[:, :])
                pe.transpose(ps_t[0:NB, 2 * P:3 * P], y[:, g, SEQ:], ident[:, :]).then_inc(v_turned, 1)

            def mix(g):
                pe.wait_ge(v_copied, 2 * g + 2)
                if g == 0:
                    pe.wait_ge(ws_ready, 2)
                    pe.wait_ge(ln_scaled, 1)
                else:
                    pe.wait_ge(mix_ready, g)
                for c in range(QT):
                    mm = pe.matmul(ps_v[:, P * c:P * c + P], vt[:, g % 2, c, :], ws_t[:, g, :], start=True, stop=True)
                mm.then_inc(mixed, 1)

            for b in range(UNIT):
                n = N_CIN + UNIT + b
                for q in range(NQ):
                    quarter(n, n % 2, q, hhi, hlo)
                    if (b, q) == (0, 0):
                        pe.wait_ge(v_summed, PAIRS)
                        statistic(acc_post)
                    if (b, q) == (1, 3):
                        pe.wait_ge(sq_used, SQ_LN + PAIRS)
                        statistic(acc_pre)
                    g = group_at(b, q)
                    if 0 < g <= CH:
                        mix(g - 1)
                    if 0 <= g < CH:
                        v_tokens(g)
            product(N_COUT, ahi, alo, gated_operand)
            post_statistic(2)
            ffn(1, N_FFN[1])


def rope_tables():
    half = HD // 2
    inv_freq = (10000.0 ** (-np.arange(half) / half)).astype(np.float32)
    pos = np.concatenate([np.arange(SEQ), np.full(NB, 2048)]).astype(np.float32)
    ang = (pos[None, :] * inv_freq[:, None]).astype(np.float32).astype(np.float64)
    c, s = np.cos(ang), np.sin(ang)
    return (np.concatenate([c, c, c, c]).astype(np.float32),
            np.concatenate([-s, s, -s, s]).astype(np.float32))


_INS = ['x_prompt', 'x_sample', 'cache_k_win', 'cache_v_win', 'state_conv', 'w_in_even', 'w_out_even', 'conv_w',
        'attn_sinks', 'w_in_cmlp', 'w_out_cmlp', 'ln_v_g', 'ln_v_b', 'w_spatial', 'b_spatial', 'w_ffn_up',
        'w_ffn_down', 'g_mix_pre', 'g_mix_post', 'g_ffn_pre', 'g_ffn_post']
_OUTS = [('y_prompt', (1, SEQ, D)), ('y_sample', (NB, 1, D)), ('new_k_win_prompt', (1, 1, WIN, NKV, HD)),
         ('new_v_win_prompt', (1, 1, WIN, NKV, HD)), ('new_conv_prompt', (1, 1, 2, CONV)),
         ('new_cmlp_v_prompt', (1, 1, P, D)), ('new_k_win_sample', (1, NB, WIN, NKV, HD)),
         ('new_v_win_sample', (1, NB, WIN, NKV, HD)), ('new_conv_sample', (1, NB, 2, CONV)),
         ('new_cmlp_v_sample', (1, NB, 1, D))]


def kernel(**inputs):
    import concourse.bacc as _bacc
    from concourse.bass_utils import run_bass_kernel_spmd as _run

    nc = _bacc.Bacc("TRN2", target_bir_lowering=False, num_devices=1, dynamic_dma_scratch_size=1024)
    arrays, io = {}, {}
    named = {name: np.ascontiguousarray(inputs[name]) for name in _INS}
    named["rope_cos"], named["rope_sin"] = rope_tables()
    for name, a in named.items():
        arrays[f"in_{name}_dram"] = a
        io[name] = nc.dram_tensor(f"in_{name}_dram", a.shape, mybir.dt.from_np(a.dtype), kind="ExternalInput").ap()
    for name, shape in _OUTS:
        io[name] = nc.dram_tensor(f"out_{name}_dram", shape, F32, kind="ExternalOutput").ap()
    build(nc, io)
    r = _run(nc, [arrays], core_ids=[0])
    return tuple(r.results[0][f"out_{name}_dram"] for name, _ in _OUTS)
```
